# Optimizing a Trainium2 kernel written in Bass

```python
import jax, jax.numpy as jnp
from jax import lax
import numpy as np

D_MODEL = 1024
BATCH = 1
SEQ = 512
DEPTH = 2
DEC_BATCH = 8
DEC_SEQ = 4
PAST_LEN = 4096
PAGE_SIZE = 128

N_MIXERS = 2
N_POOL = (DEPTH + 1) // 2
N_DN = DEPTH // 2
POOL_WINDOWS = (2, 4, 8, 16)
N_POOL_GROUPS = len(POOL_WINDOWS)
POOL_GROUP = D_MODEL // N_POOL_GROUPS
POOL_MAX = max(POOL_WINDOWS)
DK = 128
DV = 128
HK = D_MODEL // 128
HV = 2 * HK
KEY_DIM = HK * DK
VAL_DIM = HV * DV
CONV_W = 4
CONV_DIM = 2 * KEY_DIM + VAL_DIM
IN_DIM = CONV_DIM + VAL_DIM + 2 * HV
CHUNK = 64
D_FF = 2816
EPS = 1e-6

kernel_name = 'hybrid_pool_deltanet_macaron_step'

def rmsnorm(x, g):
    xf = x.astype(jnp.float32)
    y = xf * lax.rsqrt(jnp.mean(xf * xf, axis=-1, keepdims=True) + EPS) * g.astype(jnp.float32)
    return y.astype(x.dtype)

def l2norm(x):
    return x * lax.rsqrt(jnp.sum(x * x, axis=-1, keepdims=True) + EPS)

def swiglu(h, w_gate, w_up, w_down):
    return (jax.nn.silu(h @ w_gate) * (h @ w_up)) @ w_down

def pool_mixer(h, past, pos0, w_group, scale):
    B, S, D = h.shape
    P = POOL_MAX - 1
    hp = jnp.concatenate([past.astype(h.dtype), h], axis=1)
    cs = jnp.cumsum(hp.astype(jnp.float32), axis=1)
    cs = jnp.pad(cs, ((0, 0), (1, 0), (0, 0)))
    pos = pos0 + jnp.arange(S)
    groups = []
    for gi, w in enumerate(POOL_WINDOWS):
        lo, hi = gi * POOL_GROUP, (gi + 1) * POOL_GROUP
        win = cs[:, P + 1:P + 1 + S, lo:hi] - cs[:, P + 1 - w:P + 1 - w + S, lo:hi]
        cnt = jnp.minimum(pos + 1, w).astype(jnp.float32)[None, :, None]
        groups.append(win / cnt)
    pooled = jnp.concatenate(groups, axis=-1) - h.astype(jnp.float32)
    pooled = pooled.reshape(B, S, N_POOL_GROUPS, POOL_GROUP)
    y = jnp.einsum('bsgc,gcd->bsgd', pooled, w_group.astype(jnp.float32)).reshape(B, S, D)
    y = y * scale.astype(jnp.float32)
    return y.astype(h.dtype), hp[:, -P:]

def short_conv(u, past, w):
    S = u.shape[1]
    up = jnp.concatenate([past.astype(u.dtype), u], axis=1)
    out = up[:, 0:S] * w[0]
    for j in range(1, CONV_W):
        out = out + up[:, j:j + S] * w[j]
    return jax.nn.silu(out), up[:, -(CONV_W - 1):]

def chunk_gated_delta(q, k, v, beta, g, s0):
    B, S, H, _ = q.shape
    C = CHUNK if S >= CHUNK else S
    pad = (-S) % C
    if pad:
        q, k, v = [jnp.pad(t, ((0, 0), (0, pad), (0, 0), (0, 0))) for t in (q, k, v)]
        beta, g = [jnp.pad(t, ((0, 0), (0, pad), (0, 0))) for t in (beta, g)]
    N = (S + pad) // C

    def chunks(t):
        t = jnp.moveaxis(t, 2, 1)
        return t.reshape((B, H, N, C) + t.shape[3:])

    q, k, v, beta, g = [chunks(t) for t in (q, k, v, beta, g)]
    gc = jnp.cumsum(g, axis=-1)
    causal = jnp.tril(jnp.ones((C, C), dtype=bool))
    strict = jnp.tril(jnp.ones((C, C), dtype=bool), -1)
    decay = jnp.exp(jnp.where(causal, gc[..., :, None] - gc[..., None, :], -jnp.inf))
    kb = k * beta[..., None]
    vb = v * beta[..., None]
    lower = jnp.where(strict, jnp.einsum('bhnid,bhnjd->bhnij', kb, k) * decay, 0.0)
    eye = jnp.eye(C, dtype=jnp.float32)
    a_mat = eye + lower
    t_mat = lax.linalg.triangular_solve(a_mat, jnp.broadcast_to(eye, a_mat.shape),
                                        left_side=True, lower=True, unit_diagonal=True)
    u = jnp.einsum('bhnij,bhnje->bhnie', t_mat, vb)
    w = jnp.einsum('bhnij,bhnjd->bhnid', t_mat, kb * jnp.exp(gc)[..., None])
    attn = jnp.einsum('bhnid,bhnjd->bhnij', q, k) * decay
    xs = [jnp.moveaxis(t, 2, 0) for t in (q, k, u, w, gc, attn)]

    def step(state, inp):
        qi, ki, ui, wi, gi, ai = inp
        v_new = ui - jnp.einsum('bhcd,bhde->bhce', wi, state)
        o = (jnp.einsum('bhcd,bhde->bhce', qi * jnp.exp(gi)[..., None], state)
             + jnp.einsum('bhcj,bhje->bhce', ai, v_new))
        g_last = gi[..., -1]
        k_dec = ki * jnp.exp(g_last[..., None] - gi)[..., None]
        state = state * jnp.exp(g_last)[..., None, None] + jnp.einsum('bhcd,bhce->bhde', k_dec, v_new)
        return state, o

    s_final, o = lax.scan(step, s0, xs)
    o = jnp.moveaxis(o, 0, 2).reshape(B, H, N * C, -1)
    o = jnp.moveaxis(o, 1, 2)[:, :S]
    return o, s_final

def gated_deltanet(h, conv_past, s0, w_in, conv_w, a_log, dt_bias, norm_w, w_out):
    B, S, _ = h.shape
    proj = h @ w_in
    qkv_raw = proj[..., :CONV_DIM]
    z = proj[..., CONV_DIM:CONV_DIM + VAL_DIM]
    b = proj[..., CONV_DIM + VAL_DIM:CONV_DIM + VAL_DIM + HV]
    a = proj[..., CONV_DIM + VAL_DIM + HV:]
    qkv, new_conv = short_conv(qkv_raw, conv_past, conv_w)
    qkv = qkv.astype(jnp.float32)
    q = l2norm(qkv[..., :KEY_DIM].reshape(B, S, HK, DK))
    k = l2norm(qkv[..., KEY_DIM:2 * KEY_DIM].reshape(B, S, HK, DK))
    v = qkv[..., 2 * KEY_DIM:].reshape(B, S, HV, DV)
    q = jnp.repeat(q, HV // HK, axis=2) * (DK ** -0.5)
    k = jnp.repeat(k, HV // HK, axis=2)
    beta = jax.nn.sigmoid(b.astype(jnp.float32))
    g = -jnp.exp(a_log.astype(jnp.float32)) * jax.nn.softplus(a.astype(jnp.float32) + dt_bias.astype(jnp.float32))
    o, s_new = chunk_gated_delta(q, k, v, beta, g, s0.astype(jnp.float32))
    o = rmsnorm(o, norm_w) * jax.nn.silu(z.astype(jnp.float32).reshape(B, S, HV, DV))
    y = o.reshape(B, S, VAL_DIM).astype(h.dtype) @ w_out
    return y, new_conv, s_new.astype(s0.dtype)

def trunk(x, st_pool, st_conv, st_delta, pos0, p):
    new_pool, new_conv, new_delta = [], [], []
    for i in range(DEPTH):
        ng = p['norm_gains'][i]
        x = x + 0.5 * rmsnorm(swiglu(rmsnorm(x, ng[0]), p['w_ffn_gate'][i, 0],
                                     p['w_ffn_up'][i, 0], p['w_ffn_down'][i, 0]), ng[1])
        h = rmsnorm(x, ng[2])
        j = i // N_MIXERS
        if i % N_MIXERS == 0:
            y, ps = pool_mixer(h, st_pool[j], pos0, p['pool_w'][j], p['pool_scale'][j])
            new_pool.append(ps)
        else:
            y, cs, ds = gated_deltanet(h, st_conv[j], st_delta[j], p['dn_w_in'][j], p['dn_conv_w'][j],
                                       p['dn_a_log'][j], p['dn_dt_bias'][j], p['dn_norm_w'][j],
                                       p['dn_w_out'][j])
            new_conv.append(cs)
            new_delta.append(ds)
        x = x + rmsnorm(y, ng[3])
        x = x + 0.5 * rmsnorm(swiglu(rmsnorm(x, ng[4]), p['w_ffn_gate'][i, 1],
                                     p['w_ffn_up'][i, 1], p['w_ffn_down'][i, 1]), ng[5])
    return x, jnp.stack(new_pool), jnp.stack(new_conv), jnp.stack(new_delta)

def setup_inputs(seed: int = 0) -> dict:
    key = jax.random.key(seed)
    ks = jax.random.split(key, 20)
    f32 = jnp.float32
    nrm = lambda k, shape, s: jax.random.normal(k, shape, f32) * s
    x_prompt = nrm(ks[0], (BATCH, SEQ, D_MODEL), 1.0)
    x_sample = nrm(ks[1], (DEC_BATCH, DEC_SEQ, D_MODEL), 1.0)
    state_pool = nrm(ks[2], (N_POOL, DEC_BATCH, POOL_MAX - 1, D_MODEL), 1.0)
    state_conv = nrm(ks[3], (N_DN, DEC_BATCH, CONV_W - 1, CONV_DIM), 1.0)
    state_delta = nrm(ks[4], (N_DN, DEC_BATCH, HV, DK, DV), 0.05)
    norm_gains = 1.0 + nrm(ks[5], (DEPTH, 6, D_MODEL), 0.02)
    w_ffn_gate = nrm(ks[6], (DEPTH, 2, D_MODEL, D_FF), D_MODEL ** -0.5)
    w_ffn_up = nrm(ks[7], (DEPTH, 2, D_MODEL, D_FF), D_MODEL ** -0.5)
    w_ffn_down = nrm(ks[8], (DEPTH, 2, D_FF, D_MODEL), D_FF ** -0.5)
    pool_w = nrm(ks[9], (N_POOL, N_POOL_GROUPS, POOL_GROUP, POOL_GROUP), POOL_GROUP ** -0.5)
    pool_scale = 1.0 + nrm(ks[10], (N_POOL, D_MODEL), 0.1)
    dn_w_in = nrm(ks[11], (N_DN, D_MODEL, IN_DIM), D_MODEL ** -0.5)
    dn_conv_w = nrm(ks[12], (N_DN, CONV_W, CONV_DIM), CONV_W ** -0.5)
    dn_a_log = jnp.log(jax.random.uniform(ks[13], (N_DN, HV), f32, 1.0, 16.0))
    dt = jnp.exp(jax.random.uniform(ks[14], (N_DN, HV), f32, np.log(1e-3), np.log(1e-1)))
    dn_dt_bias = dt + jnp.log(-jnp.expm1(-dt))
    dn_norm_w = 1.0 + nrm(ks[15], (N_DN, DV), 0.02)
    dn_w_out = nrm(ks[16], (N_DN, VAL_DIM, D_MODEL), VAL_DIM ** -0.5)
    return {'x_prompt': x_prompt, 'x_sample': x_sample, 'state_pool': state_pool,
            'state_conv': state_conv, 'state_delta': state_delta, 'norm_gains': norm_gains,
            'w_ffn_gate': w_ffn_gate, 'w_ffn_up': w_ffn_up, 'w_ffn_down': w_ffn_down,
            'pool_w': pool_w, 'pool_scale': pool_scale, 'dn_w_in': dn_w_in, 'dn_conv_w': dn_conv_w,
            'dn_a_log': dn_a_log, 'dn_dt_bias': dn_dt_bias, 'dn_norm_w': dn_norm_w, 'dn_w_out': dn_w_out}

def reference(x_prompt, x_sample, state_pool, state_conv, state_delta, norm_gains, w_ffn_gate,
              w_ffn_up, w_ffn_down, pool_w, pool_scale, dn_w_in, dn_conv_w, dn_a_log, dn_dt_bias,
              dn_norm_w, dn_w_out):
    p = {'norm_gains': norm_gains, 'w_ffn_gate': w_ffn_gate, 'w_ffn_up': w_ffn_up,
         'w_ffn_down': w_ffn_down, 'pool_w': pool_w, 'pool_scale': pool_scale, 'dn_w_in': dn_w_in,
         'dn_conv_w': dn_conv_w, 'dn_a_log': dn_a_log, 'dn_dt_bias': dn_dt_bias,
         'dn_norm_w': dn_norm_w, 'dn_w_out': dn_w_out}
    zp = jnp.zeros((N_POOL, BATCH, POOL_MAX - 1, D_MODEL), x_prompt.dtype)
    zc = jnp.zeros((N_DN, BATCH, CONV_W - 1, CONV_DIM), x_prompt.dtype)
    zd = jnp.zeros((N_DN, BATCH, HV, DK, DV), state_delta.dtype)
    y_prompt, pool_p, conv_p, delta_p = trunk(x_prompt, zp, zc, zd, 0, p)
    y_sample, pool_s, conv_s, delta_s = trunk(x_sample, state_pool, state_conv, state_delta, PAST_LEN, p)
    return (y_prompt, y_sample, pool_p, conv_p, delta_p, pool_s, conv_s, delta_s)


_drawn_inputs = setup_inputs


def setup_inputs(seed=0):
    import zlib

    import numpy as np

    out = dict(_drawn_inputs(seed))
    spreads = {}
    factors = {}
    for name, (base, spread) in spreads.items():
        noise = np.random.default_rng([zlib.crc32(name.encode()), seed]).standard_normal(out[name].shape)
        drawn = base * np.exp(spread * noise) if base else spread * noise
        out[name] = __import__('jax').numpy.asarray(drawn.astype(out[name].dtype))
    for name, factor in factors.items():
        out[name] = (out[name] * factor).astype(out[name].dtype)
    return out
```

```python
import concourse.bass as bass
from concourse import mybir
from contextlib import ExitStack
import numpy as np

P = 128
D = 1024
KT = D // P
SEQ, NB, NS = 512, 8, 4
T = SEQ + NB * NS
HT = T // 2
FF = 2816
MF = FF // 2 // P
HK, HV, DK = 8, 16, 128
CONV_DIM = 2 * HK * DK + HV * DK
CT = CONV_DIM // P
ZT = HV
CW = 4
POOLP = 15
EPS = 1e-6

FFN_UNITS = 2 * (2 * MF + KT)
IN_UNITS = CT + ZT + 1
OUT_UNITS = 2 * KT
IN_BASE = 3 * FFN_UNITS
OUT_BASE = IN_BASE + IN_UNITS
FFN_BASE = [0, FFN_UNITS, 2 * FFN_UNITS, OUT_BASE + OUT_UNITS]


SUBLAYERS = 6
HP = POOLP + SEQ + NB * (POOLP + NS)
HTAIL = POOLP + NB * NS


LEVELS = 6
CHUNKS = SEQ // P
HQ = 4
UB = CW - 1 + SEQ + NB * (CW - 1 + NS)
CTAIL = CW - 1 + NB * NS
G, GC, KDEC, NBE, BETA = range(5)


def unit_shape(unit):
    if IN_BASE <= unit < OUT_BASE:
        return KT, (P if unit < OUT_BASE - 1 else 2 * HV)
    if OUT_BASE <= unit < OUT_BASE + OUT_UNITS:
        return KT, P
    k = (unit - (0 if unit < IN_BASE else FFN_BASE[3])) % (FFN_UNITS // 2)
    return (KT if k < 2 * MF else MF), P


def slot(unit):
    return unit % 2


def visit(unit):
    return unit // 2


def cols(hf):
    return slice(hf * HT, (hf + 1) * HT)


class Staged:

    def __init__(self, k, q, v):
        self.k, self.q, self.v = k, q, v


class Group:

    def __init__(self, rows, levels):
        self.rows, self.levels = rows, levels


def build(nc, consts, I, O):
    F = mybir.dt.float32
    R = mybir.dt.float32r
    ACT = mybir.ActivationFunctionType
    ALU = mybir.AluOpType
    ctx = ExitStack()
    with ctx:
        def sb(name, shape, dt=F, scope=ctx):
            return scope.enter_context(nc.sbuf_tensor(name, shape, dt))

        def sem(name):
            return ctx.enter_context(nc.semaphore(name))

        x = sb("x", [P, KT, T])
        y = sb("y", [P, KT, T])
        wraw = [sb(f"wraw{s}", [P, MF, P]) for s in range(2)]
        whi = [sb(f"whi{s}", [P, MF, P], R) for s in range(2)]
        wlo = [sb(f"wlo{s}", [P, MF, P], R) for s in range(2)]
        cst = sb("cst", [P, consts.shape[1]])
        ident = cst[:, 0:128]
        ones_mean = cst[:, 128:256]
        fix = cst[:, 256:256 + 64].rearrange("p (g t) -> p g t", g=4)
        ones = cst[:, 320:448]
        upto = cst[:, 448:576]
        future = cst[:, 576:704]
        strict = cst[:, 704:832]
        minus_pairs = cst[:, 832:960]
        partner = [cst[:, 960 + 64 * n:1024 + 64 * n] for n in range(LEVELS)]
        upto4 = cst[0:32, 1344:1376]
        same4 = cst[0:32, 1376:1408]
        future4 = cst[0:32, 1408:1440]
        seq_rows = cst[0:32, 1440:1448]
        gains = sb("gains", [P, 128])
        gpost = sb("gpost", [P, 4, KT])
        eps = sb("eps", [P, 1])
        ssacc = sb("ssacc", [P, 2, HT])
        sqt = sb("sqt", [P, 2, HT])
        rt = sb("rt", [P, 2, HT])
        rpre = sb("rpre", [P, 2, HT])
        rpost = sb("rpost", [P, 2, HT])

        gates = sb("gates", [P, 5, CHUNKS + 1, HV])
        acc = [ctx.enter_context(nc.psum_tensor(f"acc{s}", [P, 2, 512], F)) for s in range(2)]
        aux = [ctx.enter_context(nc.psum_tensor(f"aux{b}", [P, 512], F)) for b in range(4)]

        def gain(layer, i, k):
            c = (layer * 6 + i) * KT + k
            return gains[:, c:c + 1]

        const_in = sem("const_in")
        rows_in = sem("rows_in")
        tok_in = sem("tok_in")
        raw_full = [sem(f"raw_full{s}") for s in range(2)]
        w_hi = [sem(f"w_hi{s}") for s in range(2)]
        w_lo = [sem(f"w_lo{s}") for s in range(2)]
        acc_done = [sem(f"acc_done{s}") for s in range(2)]
        taken = [sem(f"taken{s}") for s in range(2)]
        setup_done = sem("setup_done")
        aux_done = sem("aux_done")
        aux_taken = sem("aux_taken")
        x_ready = sem("x_ready")
        x_sq = sem("x_sq")
        ms_done = sem("ms_done")
        rt_done = sem("rt_done")
        rb_ready = sem("rb_ready")
        h_hi = sem("h_hi")
        h_lo = sem("h_lo")
        gate_silu = sem("gate_silu")
        hid_ready = sem("hid_ready")
        hid_hi = sem("hid_hi")
        hid_lo = sem("hid_lo")
        y_sq = sem("y_sq")
        ss_acc = sem("ss_acc")
        y_norm = sem("y_norm")
        out_copied = sem("out_copied")
        conv_in = sem("conv_in")
        conv_pads = sem("conv_pads")
        tap0 = [sem(f"tap0_{s}") for s in range(2)]
        conv_done = [sem(f"conv_done{s}") for s in range(2)]
        silu_done = [sem(f"silu_done{s}") for s in range(2)]
        zv_stored = [sem(f"zv_stored{s}") for s in range(2)]
        nq_sq = sem("nq_sq")
        nq_ms = sem("nq_ms")
        nq_ln = sem("nq_ln")
        nq_rs = sem("nq_rs")
        nq_done = sem("nq_done")
        qk_stored = sem("qk_stored")
        ba_ready = sem("ba_ready")
        g_step = sem("g_step")
        g_act = sem("g_act")
        g_sum = sem("g_sum")
        gates_ready = sem("gates_ready")
        conv_stored = sem("conv_stored")
        def sem2(name):
            return [sem(f"{name}_{q}") for q in range(2)]
        stage_in = [sem2(f"stage_in{p}") for p in range(2)]
        stage_in_s = sem2("stage_in_s")
        gate_in = sem2("gate_in")
        gtri_r = sem("gtri_r")
        kk_ps = sem("kk_ps")
        gcb_ps = sem("gcb_ps")
        kv_ps = sem("kv_ps")
        dec_sub = sem("dec_sub")
        dec_exp = sem("dec_exp")
        eg_exp = sem("eg_exp")
        att_r = sem("att_r")
        kd_r = sem("kd_r")
        low_r = sem("low_r")
        beta_r = sem2("beta_r")
        t0a = sem2("t0a")
        t0 = sem2("t0")
        tr_ps = sem2("tr_ps")
        att_c = sem("att_c")
        u_c = sem("u_c")
        kdec_r = sem("kdec_r")
        vb_r = sem("vb_r")
        kq_k = sem2("kq_k")
        kq_ps = sem("kq_ps")
        ks_c = sem("ks_c")
        ks_ps = sem2("ks_ps")
        ks_r = sem2("ks_r")
        rv_r = sem2("rv_r")
        y_ps = sem2("y_ps")
        y_r = sem2("y_r")
        ut_ps = sem2("ut_ps")
        ut_r = sem2("ut_r")
        vn_ps = sem2("vn_ps")
        vn_c = sem2("vn_c")
        vnm_r = sem2("vnm_r")
        qd_r = sem2("qd_r")
        o_ps = sem2("o_ps")
        o_c = sem2("o_c")
        o_stored = sem2("o_stored")
        ds_ps = sem2("ds_ps")
        sd_r = sem2("sd_r")
        ds_s = sem("ds_s")
        sd_s = sem("sd_s")
        sn_s = sem("sn_s")
        group_done = sem2("group_done")
        sample_go = sem("sample_go")
        s_stored = sem("s_stored")
        of_in = [sem(f"of_in{b}") for b in range(2)]
        z_silu = sem("z_silu")
        on_sq = sem("on_sq")
        on_ms = sem("on_ms")
        on_ln = sem("on_ln")
        on_rs = sem("on_rs")
        on_norm = sem("on_norm")
        on_gate = sem("on_gate")
        o_hi = sem("o_hi")
        o_lo = sem("o_lo")
        past_in = sem("past_in")
        poolw_in = sem("poolw_in")
        hp_ready = sem("hp_ready")
        tail_ready = sem("tail_ready")
        win_dve = sem("win_dve")
        win_pool = sem("win_pool")
        pooled_ready = sem("pooled_ready")
        pool_mm = sem("pool_mm")
        pool_y = sem("pool_y")
        pool_stored = sem("pool_stored")
        ss_zero = sem("ss_zero")
        stored = sem("stored")

        with ExitStack() as sc:
            hhi = sb("hhi", [P, KT, T], R, sc)
            hlo = sb("hlo", [P, KT, T], R, sc)
            with ExitStack() as s2:
                hidhi = sb("hidhi", [P, MF, T], R, s2)
                hidlo = sb("hidlo", [P, MF, T], R, s2)
                tmpg = sb("tmpg", [P, 2, HT], F, s2)
                sil = sb("sil", [P, 2, HT], F, s2)
                tmpu = sb("tmpu", [P, 2, HT], F, s2)
                hidf = sb("hidf", [P, 2, HT], F, s2)
            with ExitStack() as s2:
                xt = sb("xt", [P, 5, D], F, s2)
                rows = sb("rows", [P, P], F, s2)
        with ExitStack() as sc:
            hp = sb("hp", [P, KT, HP], F, sc)
            winv = [sb(f"winv{b}", [P, 2, HP], F, sc) for b in range(2)]
            winp = [sb(f"winp{b}", [P, 2, HP], F, sc) for b in range(2)]
            pooled = sb("pooled", [P, KT, T], F, sc)
            poolw = sb("poolw", [P, 8, 256], F, sc)
            past = sb("past", [NB * POOLP, D], F, sc)
            tail = sb("tail", [P, KT, HTAIL], F, sc)
            tailrows = sb("tailrows", [HTAIL, D], F, sc)
        NR = NB * NS

        def group_buffers(sc, q, rows, levels):
            def four(name, n=rows):
                return sb(f"{name}{rows}_{q}", [P, 4, n], F, sc)
            g = Group(rows, levels)
            g.gate = sb(f"gate{rows}_{q}", [P, 5, 4], F, sc)
            g.gtri, g.low, g.dec, g.att, g.kd, g.T, g.U, g.attT, g.eg, g.qd, g.oT = (
                four(n) for n in ("gtri", "low", "dec", "att", "kd", "T", "U", "attT", "eg", "qd", "oT"))
            g.kdec, g.vb, g.rv, g.vn = (four(n, P) for n in ("kdec", "vb", "rv", "vn"))
            g.Y = [four(f"Y{n}_") for n in range(levels)]
            return g

        with ExitStack() as sc:
            S = sb("S", [P, HV, P], F, sc)
            Sd = [sb(f"Sd{q}", [P, 4, P], F, sc) for q in range(2)]
            staged = [[Staged(k=sb(f"kT{p}{q}", [P, 2, P], F, sc), q=sb(f"qT{p}{q}", [P, 2, P], F, sc),
                                       v=sb(f"vT{p}{q}", [P, 4, P], F, sc)) for q in range(2)] for p in range(2)]
            GP = [group_buffers(sc, q, P, LEVELS) for q in range(2)]
        with ExitStack() as sc:
            GS = [group_buffers(sc, q, NR, 1) for q in range(2)]
            staged_s = [Staged(k=sb(f"kTs{q}", [P, 2, NR], F, sc), q=sb(f"qTs{q}", [P, 2, NR], F, sc),
                                        v=sb(f"vTs{q}", [P, 4, NR], F, sc)) for q in range(2)]
            Ss = [sb(f"Ss{q}", [P, 4, NB, P], F, sc) for q in range(2)]
            Sds = [sb(f"Sds{n}", [P, NB, P], F, sc) for n in range(2)]
            kq = [sb(f"kq{q}", [P, 4, NB, 2, NS], F, sc) for q in range(2)]
            kqS = [sb(f"kqS{q}", [P, 2, 4, NR], F, sc) for q in range(2)]
            vnm = [sb(f"vnm{q}", [NR, 4, NB, P], F, sc) for q in range(2)]
        with ExitStack() as sc:
            ohi = sb("ohi", [P, HV, T], R, sc)
            olo = sb("olo", [P, HV, T], R, sc)
            zs = [sb(f"zs{b}", [P, HQ, T], F, sc) for b in range(2)]
            of = [sb(f"of{b}", [P, HQ, T], F, sc) for b in range(2)]
        with ExitStack() as sc:
            sb("normed_input", [P, 2, KT, T], F, sc)
            qk = sb("qk", [P, 2 * HK, T], F, sc)
            ub = [sb(f"ub{s}", [P, UB], F, sc) for s in range(2)]
            conv = [sb(f"conv{s}", [P, UB], F, sc) for s in range(2)]
            zv = [sb(f"zv{s}", [P, T], F, sc) for s in range(2)]
            convrows = sb("convrows", [P, P], F, sc)
            convw = sb("convw", [P, P], F, sc)
            pastc = sb("pastc", [P, CT, NB * (CW - 1)], F, sc)
            tailc = sb("tailc", [P, CT, CTAIL], F, sc)
            crow = sb("crow", [CTAIL, CONV_DIM], F, sc)
            sqn = sb("sqn", [P, T], F, sc)
            lnn = sb("lnn", [P, T], F, sc)
            rsn = sb("rsn", [P, T], F, sc)
            ba = sb("ba", [2 * HV, T], F, sc)
            bat = sb("bat", [P, CHUNKS + 1, 2 * HV], F, sc)
            gtmp = sb("gtmp", [P, 8, CHUNKS + 1, HV], F, sc)
            alog = sb("alog", [P, HV], F, sc)
            dtb = sb("dtb", [P, HV], F, sc)

        wg = I["w_ffn_gate"].rearrange("l j k n -> (l j k) n")
        wu = I["w_ffn_up"].rearrange("l j k n -> (l j k) n")
        wd = I["w_ffn_down"].rearrange("l j k n -> (l j k) n")
        xp = I["x_prompt"].rearrange("b s d -> (b s) d")
        xs = I["x_sample"].rearrange("b s d -> (b s) d")
        WINDOWS = (2, 4, 8, 16)
        FFN_OF = [0, None, 1, 2, None, 3]
        NTH = [0, None, 1, 2, 3, 4]
        last_unit = FFN_BASE[3] + FFN_UNITS
        AUX_PAST, AUX_TAIL = 11, 13
        AUX_DN = 15
        AUX_END = AUX_DN + 12
        w_in = I["dn_w_in"].rearrange("l k n -> (l k) n")
        w_out = I["dn_w_out"].rearrange("l k n -> (l k) n")
        qk_d = nc.dram_tensor("qk_scratch", [2 * HK, P, T], F, kind="Internal").ap()
        v_d = nc.dram_tensor("v_scratch", [HV, P, T], F, kind="Internal").ap()
        z_d = nc.dram_tensor("z_scratch", [HV, P, T], F, kind="Internal").ap()
        o_d = nc.dram_tensor("o_scratch", [HV, P, T], F, kind="Internal").ap()
        banks = [[acc[0][:, 0, :], acc[0][:, 1, :], acc[1][:, 0, :], acc[1][:, 1, :]], [a[:, :] for a in aux]]
        def norm_bank(h, hf):
            return (acc[h][:, hf, :] if h < 2 else aux[2 * (h - 2) + hf][:, :])[:, 0:HT]

        def kq_bank(q):
            return banks[q][2][:, 0:4 * NB * 2 * NS].rearrange("p (h b z t) -> p h b z t", h=4, b=NB, z=2)

        TT = [(t, P) for t in range(4)] + [(4, NB * NS)]

        block = ctx.enter_context(nc.Block())

        @block.sync
        def _(sp):
            sp.dma_start(cst[:], consts).then_inc(const_in, 16)
            for t, n in TT:
                src = xp[t * P:(t + 1) * P, :] if t < 4 else xs
                sp.dma_start(xt[0:n, t, :], src).then_inc(tok_in, 16)
            sp.dma_start(rows[0:96, :], I["norm_gains"].rearrange("l i (k p) -> (l i k) p", p=P)).then_inc(rows_in, 16)
            sp.dma_start(rows[96:104, :], I["pool_scale"].rearrange("l (k p) -> (l k) p", p=P)).then_inc(rows_in, 16)
            sp.dma_start(rows[104:105, :], I["dn_norm_w"]).then_inc(rows_in, 16)

            def load(unit, i, src, nk, width=P):
                s, v = slot(unit), visit(unit)
                sp.wait_ge(w_lo[s], i + (v + 1))
                sp.dma_start(wraw[s][:, 0:nk, 0:width], src.rearrange("(k p) n -> p k n", p=P))\
                  .then_inc(raw_full[s], 16)

            def ffn(e):
                for f in range(2):
                    base = FFN_BASE[e] + f * (FFN_UNITS // 2)
                    with sp.Fori(0, MF) as i:
                        for k, w in enumerate((wg, wu)):
                            load(base + k, i, w[e * D:(e + 1) * D, bass.ds(i * P + f * MF * P, P)], KT)
                    with sp.Fori(0, KT // 2) as i:
                        for k in range(2):
                            load(base + 2 * MF + k, i,
                                 wd[e * FF + f * MF * P:e * FF + (f + 1) * MF * P, bass.ds(i * (2 * P) + k * P, P)], MF)
            def pool_mixer():
                u = FFN_BASE[1] - 1
                sp.wait_ge(acc_done[slot(u)], 2 * visit(u) + 2)
                sp.dma_start(past[:], I["state_pool"].rearrange("l b t d -> (l b t) d")).then_inc(past_in, 16)
                sp.dma_start(poolw[:], I["pool_w"].rearrange("l g (k p) d -> p (l g k) d", p=P)).then_inc(poolw_in, 16)

            def load_out(i, k):
                load(OUT_BASE + k, i, w_out[k * D:(k + 1) * D, bass.ds(i * P, P)] if not isinstance(i, int)
                     else w_out[k * D:(k + 1) * D, i * P:(i + 1) * P], KT)

            def delta_in():
                u = IN_BASE - 1
                sp.wait_ge(acc_done[slot(u)], 2 * visit(u) + 2)
                sp.dma_start(convrows[:], I["dn_conv_w"].rearrange("l j (k p) -> (l j k) p", p=P)).then_inc(conv_in, 16)
                sp.dma_start(crow[0:NB * (CW - 1), :], I["state_conv"].rearrange("l b t d -> (l b t) d")).then_inc(conv_in, 16)
                sp.dma_start(alog[:], I["dn_a_log"].broadcast_to([P, HV])).then_inc(conv_in, 16)
                sp.dma_start(dtb[:], I["dn_dt_bias"].broadcast_to([P, HV])).then_inc(conv_in, 16)
                with sp.Fori(0, (CT + ZT) // 2) as i:
                    for k in range(2):
                        load(IN_BASE + k, i, w_in[:, bass.ds(i * (2 * P) + k * P, P)], KT)
                load(OUT_BASE - 1, 0, w_in[:, (CT + ZT) * P:(CT + ZT) * P + 2 * HV], KT, 2 * HV)
                for k in range(2):
                    load_out(0, k)
                sp.wait_ge(aux_taken, AUX_DN + 12)
                sp.dma_start(O["conv_prompt"][0, 0, :, :], crow[0:CW - 1, :]).then_inc(conv_stored, 16)
                for b in range(NB):
                    sp.dma_start(O["conv_sample"][0, b, :, :], crow[CW - 1 + NS * b + 1:CW - 1 + NS * (b + 1), :])\
                      .then_inc(conv_stored, 16)
                sp.wait_ge(conv_stored, 16 * (NB + 1))

            def load_sampled(i, q):
                b, tok = staged_s[q], slice(SEQ, T)
                for dst, src, first, count in ((b.q, qk_d, i * 4 + 2 * q, 2), (b.k, qk_d, i * 4 + (HK + 2 * q), 2),
                                               (b.v, v_d, i * 8 + 4 * q, 4)):
                    sp.dma_start(dst[:, :, :], src[first:first + count, :, tok].rearrange("k p t -> p k t")).then_inc(stage_in_s[q], 16)
                for h in range(4):
                    src = I["state_delta"][0, :, i * 8 + (4 * q + h), :, :]
                    sp.dma_start(Ss[q][:, h, :, :], src.rearrange("b k v -> k b v")).then_inc(stage_in_s[q], 16)

            def delta_core():
                sp.wait_ge(qk_stored, 16 * 2 * HK)
                for s in range(2):
                    sp.wait_ge(zv_stored[s], 16 * (HV + 1))
                with sp.Fori(0, CHUNKS) as i:
                    for p in range(2):
                        for q in range(2):
                            g = 2 * p + q
                            b, tok = staged[p][q], bass.ds(i * P, P)
                            sp.wait_ge(group_done[q], i * 2 + (p + 1))
                            for dst, src in ((b.q, qk_d[2 * g:2 * g + 2, :, tok]), (b.k, qk_d[HK + 2 * g:HK + 2 * g + 2, :, tok]),
                                             (b.v, v_d[4 * g:4 * g + 4, :, tok])):
                                sp.dma_start(dst[:, :, :], src.rearrange("k p t -> p k t")).then_inc(stage_in[p][q], 16)
                n = 2 * CHUNKS
                for q in range(2):
                    sp.wait_ge(group_done[q], n + 2)
                    sp.wait_ge(o_stored[q], 16 * (n + 1))
                sp.dma_start(O["delta_prompt"][0, 0].rearrange("h k v -> k h v"), S[:, :, :]).then_inc(s_stored, 16)
                sp.wait_ge(s_stored, 16)
                sp.sem_inc(sample_go, 1)
                for q in range(2):
                    load_sampled(0, q)
                for i in range(2):
                    for q in range(2):
                        sp.wait_ge(group_done[q], i + (n + 3))
                        for h in range(4):
                            dst = O["delta_sample"][0, :, i * 8 + (4 * q + h), :, :]
                            sp.dma_start(dst.rearrange("b k v -> k b v"), Ss[q][:, h, :, :]).then_inc(s_stored, 16)
                        sp.wait_ge(s_stored, 16 + 64 * (2 * i + q + 1))
                        if i == 0:
                            load_sampled(1, q)
                for q in range(2):
                    sp.wait_ge(o_stored[q], 16 * (n + 3))
                for j in range(HV // HQ):
                    if j >= 2:
                        sp.wait_ge(o_lo, j - 1)
                    for dst, src in ((of[j % 2], o_d), (zs[j % 2], z_d)):
                        sp.dma_start(dst[:, :, :], src[HQ * j:HQ * (j + 1), :, :].rearrange("h p t -> p h t")).then_inc(of_in[j % 2], 16)
                with sp.Fori(1, KT) as i:
                    for k in range(2):
                        load_out(i, k)

            ffn(0)
            pool_mixer()
            ffn(1)
            ffn(2)
            delta_in()
            delta_core()
            ffn(3)
            for t, n in TT:
                sp.wait_ge(out_copied, 2 * t + 2)
                dst = O["y_prompt"].rearrange("b s d -> (b s) d")[t * P:(t + 1) * P, :] if t < 4 \
                    else O["y_sample"].rearrange("b s d -> (b s) d")
                sp.dma_start(dst, xt[0:n, t, :]).then_inc(stored, 16)
            sp.wait_ge(stored, 16 * 5)
            sp.wait_ge(pool_stored, 16 * 10)
        @block.gpsimd
        def _(pool):
            def split(unit, i):
                s, v = slot(unit), visit(unit)
                nk, width = unit_shape(unit)
                pool.wait_ge(w_hi[s], i + (v + 1))
                pool.tensor_tensor(wlo[s][:, 0:nk, 0:width], wraw[s][:, 0:nk, 0:width],
                                   whi[s][:, 0:nk, 0:width].bitcast(F), ALU.subtract).then_inc(w_lo[s], 1)

            for s in range(2):
                pool.sem_inc(w_lo[s], 1)

            def ffn(e):
                for f in range(2):
                    base = FFN_BASE[e] + f * (FFN_UNITS // 2)
                    with pool.Fori(0, MF) as i:
                        for k in range(2):
                            split(base + k, i)
                    with pool.Fori(0, KT // 2) as i:
                        for k in range(2):
                            split(base + 2 * MF + k, i)

            def pool_mixer():
                src = hp[:, 6:8, :]
                pool.wait_ge(hp_ready, KT + 3)
                for j in range(4):
                    w, dst = 1 << j, winp[j % 2]
                    if j:
                        pool.wait_ge(win_pool, j)
                    pool.tensor_tensor(dst[:, :, 2 * w - 1:HP], src[:, :, 2 * w - 1:HP], src[:, :, w - 1:HP - w], ALU.add)\
                        .then_inc(win_pool, 1)
                    src = dst

            def decay_start(q, n, g):
                r = g.rows
                pool.wait_ge(gate_in[q], n + 1)
                tri = (upto if r == P else upto4).unsqueeze(1).broadcast_to([r, 4, r])
                pool.tensor_tensor(g.gtri[0:r], tri, g.gate[0:r, G, :].unsqueeze(2).broadcast_to([r, 4, r]), ALU.mult)\
                    .then_inc(gtri_r, 1)

            def strict_beta(q, n, g):
                r = g.rows
                pool.tensor_tensor(g.low[0:r], strict[0:r, 0:r].unsqueeze(1).broadcast_to([r, 4, r]),
                                   g.gate[0:r, BETA, :].unsqueeze(2).broadcast_to([r, 4, r]), ALU.mult).then_inc(beta_r[q], 1)

            def lower(n, g):
                r = g.rows
                pool.wait_ge(low_r, n * 2 + 1)
                pool.tensor_tensor(g.kd[0:r], g.low[0:r], minus_pairs[0:r, 0:r].unsqueeze(1).broadcast_to([r, 4, r]), ALU.mult)\
                    .then_inc(t0a[0], 1)
                pool.wait_ge(t0a[0], n + 1)
                pool.tensor_tensor(g.T[0:r], g.kd[0:r], ident[0:r, 0:r].unsqueeze(1).broadcast_to([r, 4, r]), ALU.add)\
                    .then_inc(t0[0], 1)

            def right_side(q, n, g):
                r = g.rows
                pool.wait_ge(vb_r, n * 2 + (q + 1))
                pool.wait_ge(ks_r[q], n + 1)
                pool.tensor_tensor(g.rv[0:r], g.rv[0:r], g.vb[0:r], ALU.add).then_inc(rv_r[q], 1)

            def decayed_queries(q, n, g, b):
                pool.wait_ge(eg_exp, n * 2 + (q + 1))
                pool.tensor_tensor(g.qd[:, :, :].rearrange("p (k v) i -> p k v i", k=2),
                                   b.q[:, :, :].unsqueeze(2).broadcast_to([P, 2, 2, g.rows]),
                                   g.eg[:, :, :].rearrange("p (k v) i -> p k v i", k=2), ALU.mult).then_inc(qd_r[q], 1)

            def delta_core():
                for k in range(2):
                    split(OUT_BASE + k, 0)
                with pool.Fori(0, CHUNKS) as i:
                    for p in range(2):
                        n = lambda: i * 2 + p
                        for q in range(2):
                            decay_start(q, n(), GP[q])
                        for q in range(2):
                            strict_beta(q, n(), GP[q])
                        lower(n(), GP[0])
                        for q in range(2):
                            decayed_queries(q, n(), GP[q], staged[p][q])
                            right_side(q, n(), GP[q])
                        for q in range(2):
                            hs = slice(4 * (2 * p + q), 4 * (2 * p + q) + 4)
                            pool.tensor_tensor(Sd[q][:, :, :], S[:, hs, :], GP[q].eg[:, :, P - 1:P].broadcast_to([P, 4, P]), ALU.mult)\
                                .then_inc(sd_r[q], 1)
                pool.wait_ge(sample_go, 1)
                pool.sem_inc(sd_s, 2)
                with pool.Fori(0, 2) as i:
                    m = 2 * CHUNKS
                    for q in range(2):
                        decay_start(q, i + m, GS[q])
                    for q in range(2):
                        strict_beta(q, i + m, GS[q])
                    lower(i + m, GS[0])
                    for q in range(2):
                        pool.wait_ge(stage_in_s[q], i * 112 + 112)
                        pool.wait_ge(eg_exp, (i + m) * 2 + (q + 1))
                        for v in range(2):
                            last = pool.tensor_tensor(kq[q][:, v::2, :, 1, :], staged_s[q].q[:, :, :].rearrange("p k (b t) -> p k b t", b=NB),
                                                      GS[q].eg[:, v::2, :].rearrange("p k (b t) -> p k b t", b=NB), ALU.mult)
                        last.then_inc(qd_r[q], 1)
                    for q in range(2):
                        right_side(q, i + m, GS[q])
                    for q in range(2):
                        for h in range(4):
                            j = 4 * q + h
                            pool.wait_ge(sn_s, i * 16 + 2 * j)
                            last_cols = GS[q].eg[:, h, :].rearrange("p (b t) -> p b t", b=NB)[:, :, NS - 1:NS]
                            pool.tensor_tensor(Sds[h % 2][:], Ss[q][:, h, :, :], last_cols.broadcast_to([P, NB, P]), ALU.mult)\
                                .then_inc(sd_s, 1)
                for j in range(HV // HQ):
                    pool.wait_ge(of_in[j % 2], 32 * (j // 2 + 1))
                    if j > 0:
                        pool.wait_ge(on_ms, j)
                    pool.tensor_tensor(y[:, 0:HQ, :], of[j % 2][:, :, :], of[j % 2][:, :, :], ALU.mult).then_inc(on_sq, 1)
                with pool.Fori(1, KT) as i:
                    for k in range(2):
                        split(OUT_BASE + k, i)

            ffn(0)
            pool_mixer()
            ffn(1)
            ffn(2)
            with pool.Fori(0, (CT + ZT) // 2) as i:
                for k in range(2):
                    split(IN_BASE + k, i)
            split(OUT_BASE - 1, 0)
            delta_core()
            ffn(3)

        @block.tensor
        def _(pe):
            def unit(u, i, nk, act_hi, act_lo, k0=0, width=P, half_ready=None):
                s, v = slot(u), visit(u)
                pe.wait_ge(w_lo[s], i + (v + 2))
                for hf in range(2):
                    if half_ready is not None:
                        pe.wait_ge(*half_ready(hf))
                    pe.wait_ge(taken[s], (i + v) * 2 + hf + 1)
                    n = 0
                    for k in range(nk):
                        for w, a in ((whi, act_hi), (wlo, act_hi), (whi, act_lo)):
                            last = pe.matmul(acc[s][0:width, hf, 0:HT], w[s][:, k, 0:width], a[:, k0 + k, cols(hf)],
                                             start=(n == 0), stop=(n == 3 * nk - 1))
                            n += 1
                    last.then_inc(acc_done[s], 1)

            def pre(r):
                for hf in range(2):
                    pe.wait_ge(x_sq, 2 * r + hf + 1)
                    for k in range(KT):
                        last = pe.matmul(aux[hf][:, 0:HT], ones_mean, y[:, k, cols(hf)], start=(k == 0), stop=(k == KT - 1))
                    last.then_inc(ms_done, 1)

            def post(r):
                for hf in range(2):
                    pe.wait_ge(ss_acc, 16 * r + KT * 2 + hf)
                    pe.matmul(aux[hf][:, 0:HT], ones_mean, ssacc[:, hf, :], start=True, stop=True).then_inc(ms_done, 1)

            def ffn(e, r):
                for f in range(2):
                    base = FFN_BASE[e] + f * (FFN_UNITS // 2)
                    with pe.Fori(0, MF) as i:
                        for k in range(2):
                            unit(base + k, i, KT, hhi, hlo, half_ready=lambda hf: (h_lo, 16 * NTH[r] + 8 * (hf + 1)))
                    done = ((2 * e + f) + 1) * 2 * MF
                    with pe.Fori(0, KT // 2) as i:
                        for k in range(2):
                            unit(base + 2 * MF + k, i, MF, hidhi, hidlo, half_ready=lambda hf: (hid_lo, done - 1 + hf))

            pe.wait_ge(const_in, 16)
            pe.wait_ge(rows_in, 48)
            pe.transpose(aux[3][:, 0:105], rows[0:105, :], ident[0:105, 0:105]).then_inc(aux_done, 1)
            pe.wait_ge(tok_in, 80)
            for t, n in TT:
                for kk in range(2):
                    b = 2 * t + kk
                    if b >= 2:
                        pe.wait_ge(aux_taken, b)
                    for k in range(4):
                        last = pe.transpose(aux[b % 2][:, k * n:(k + 1) * n], xt[0:n, t, (4 * kk + k) * P:(4 * kk + k + 1) * P],
                                            ident[0:n, 0:n])
                    last.then_inc(aux_done, 1)

            def pool_mixer():
                pe.wait_ge(past_in, 16)
                for b in range(2):
                    for k in range(4):
                        last = pe.transpose(aux[2 + b][:, k * 120:(k + 1) * 120], past[:, (4 * b + k) * P:(4 * b + k + 1) * P],
                                            ident[0:120, 0:120])
                    last.then_inc(aux_done, 1)
                pre(1)
                pe.wait_ge(tail_ready, 2)
                for b in range(2):
                    pe.wait_ge(aux_taken, AUX_PAST + b + 1)
                    for k in range(4):
                        last = pe.transpose(aux[2 + b][0:HTAIL, k * P:(k + 1) * P], tail[:, 4 * b + k, :], ident)
                    last.then_inc(aux_done, 1)
                pe.wait_ge(poolw_in, 16)
                for mt in range(KT):
                    g, m = mt // 2, mt % 2
                    pe.wait_ge(pooled_ready, g + 1)
                    for hf in range(2):
                        if mt:
                            pe.wait_ge(pool_y, 2 * (mt - 1) + hf + 1)
                        else:
                            pe.wait_ge(aux_taken, AUX_TAIL + hf + 1)
                        for k in range(2):
                            last = pe.matmul(aux[2 + hf][:, 0:HT], poolw[:, 2 * g + k, m * P:(m + 1) * P],
                                             pooled[:, 2 * g + k, cols(hf)], start=(k == 0), stop=(k == 1))
                        last.then_inc(pool_mm, 1)
                post(1)

            def heads(_, rows_of, h):
                return slice(h * rows_of, (h + 1) * rows_of)

            def products(q, n, g, b, ready):
                r, (b0, b1, b2, b3) = g.rows, banks[q]
                pe.wait_ge(*ready)
                pe.wait_ge(group_done[q], n + 2)
                pe.wait_ge(o_c[q], n + 1)
                for k in range(2):
                    pe.matmul(b0[0:r, heads(g, r, k)], b.k[:, k, :], b.k[:, k, :], start=True, stop=True)
                for k in range(2):
                    last = pe.matmul(b0[0:r, heads(g, r, 2 + k)], b.q[:, k, :], b.k[:, k, :], start=True, stop=True)
                last.then_inc(kk_ps, 1)
                pe.wait_ge(gtri_r, n * 2 + (q + 1))
                pe.matmul(b1[:, 0:4 * r], ones[0:r, :], g.gtri[0:r].rearrange("p h i -> p (h i)"), start=True, stop=True)\
                  .then_inc(gcb_ps, 1)
                for k in range(2):
                    pe.transpose(b2[0:r, heads(g, P, k)], b.k[:, k, :], ident)
                for h in range(4):
                    last = pe.transpose(b3[0:r, heads(g, P, h)], b.v[:, h, :], ident)
                last.then_inc(kv_ps, 1)

            def transposes(q, n, g):
                r, (b0, b1, b2, b3) = g.rows, banks[q]
                pe.wait_ge(eg_exp, n * 2 + (q + 1))
                pe.wait_ge(att_r, n * 2 + (q + 1))
                for h in range(4):
                    last = pe.transpose(b1[0:r, heads(g, r, h)], g.att[0:r, h, :], ident[0:r, 0:r])
                last.then_inc(tr_ps[q], 1)
                pe.wait_ge(kd_r, n * 2 + (q + 1))
                pe.wait_ge(t0[q], n + 1)
                for h in range(4):
                    last = pe.transpose(b0[0:r, heads(g, r, h)], g.T[0:r, h, :], ident[0:r, 0:r])
                last.then_inc(tr_ps[q], 1)

            def halves(a, lv):
                return a.rearrange("p (b two l) -> p b two l", two=2, l=2 << lv)

            def level_y(q, nl, g, lv):
                r, (b0, b1, b2, b3) = g.rows, banks[q]
                if lv == 0:
                    pe.wait_ge(u_c, nl[0] * 2 + (q + 1))
                    pe.wait_ge(low_r, nl[0] * 2 + (q + 1))
                else:
                    pe.wait_ge(ut_r[q], nl[1] + lv)
                for h in range(4):
                    last = pe.matmul(b0[0:r, heads(g, r // 2, h)].rearrange("p (b l) -> p b l", l=2 << lv), g.low[0:r, h, :],
                                     halves(g.U[0:r, h, :], lv)[:, :, 1, :], start=True, stop=True)
                last.then_inc(y_ps[q], 1)

            def level_ut(q, nl, g, lv):
                r, (b0, b1, b2, b3) = g.rows, banks[q]
                pe.wait_ge(y_r[q], nl[1] + lv + 1)
                if lv == 0:
                    pe.wait_ge(att_c, nl[0] * 2 + (q + 1))
                for h in range(4):
                    last = pe.matmul(b1[0:r, heads(g, r // 2, h)].rearrange("p (b l) -> p b l", l=2 << lv), g.T[0:r, h, :],
                                     halves(g.Y[lv][0:r, h, :], lv)[:, :, 1, :], start=True, stop=True)
                if lv < g.levels - 1:
                    for h in range(4):
                        last = pe.matmul(b1[0:r, heads(g, r // 2, 4 + h)].rearrange("p (b l) -> p b l", l=2 << lv),
                                         g.Y[lv][0:r, h, :], halves(g.T[0:r, h, :], lv)[:, :, 0, :], start=True, stop=True)
                last.then_inc(ut_ps[q], 1)

            def new_values(q, nl, g):
                r, (b0, b1, b2, b3) = g.rows, banks[q]
                pe.wait_ge(rv_r[q], nl[0] + 1)
                pe.wait_ge(ut_r[q], nl[1] + g.levels)
                for h in range(4):
                    last = pe.matmul(b3[0:r, heads(g, P, h)], g.U[0:r, h, :], g.rv[0:r, h, :], start=True, stop=True)
                last.then_inc(vn_ps[q], 1)

            def delta_core():
                with pe.Fori(0, CHUNKS) as i:
                    for p in range(2):
                        def nl():
                            return i * 2 + p, i * 12 + 6 * p
                        for q in range(2):
                            products(q, nl()[0], GP[q], staged[p][q], (stage_in[p][q], i * 48 + 48))
                        for q in range(2):
                            transposes(q, nl()[0], GP[q])
                        for q in range(2):
                            b2 = banks[q][2]
                            pe.wait_ge(kdec_r, nl()[0] * 2 + (q + 1))
                            for h in range(4):
                                last = pe.matmul(b2[:, heads(None, P, h)], staged[p][q].k[:, h // 2, :], S[:, 4 * (2 * p + q) + h, :],
                                                 start=True, stop=True)
                            last.then_inc(ks_ps[q], 1)
                        for lv in range(LEVELS):
                            for q in range(2):
                                level_y(q, nl(), GP[q], lv)
                            for q in range(2):
                                level_ut(q, nl(), GP[q], lv)
                        for q in range(2):
                            g, b0 = GP[q], banks[q][0]
                            pe.wait_ge(qd_r[q], nl()[0] + 1)
                            for h in range(4):
                                pe.matmul(b0[:, heads(g, P, h)], S[:, 4 * (2 * p + q) + h, :], g.qd[:, h, :], start=(h == 0), stop=False)
                        for q in range(2):
                            new_values(q, nl(), GP[q])
                        for q in range(2):
                            g, (b0, b1, b2, b3) = GP[q], banks[q]
                            pe.wait_ge(vn_c[q], nl()[0] + 1)
                            for h in range(4):
                                last = pe.matmul(b1[:, heads(g, P, h)], g.kdec[:, h, :], g.vn[:, h, :], start=True, stop=True)
                            last.then_inc(ds_ps[q], 1)
                            for h in range(4):
                                last = pe.matmul(b0[:, heads(g, P, h)], g.vn[:, h, :], g.attT[:, h, :], start=False, stop=(h == 3))
                            last.then_inc(o_ps[q], 1)
                pe.wait_ge(sample_go, 1)
                for i in range(2):
                    def nl():
                        return i + 2 * CHUNKS, i + 2 * CHUNKS * LEVELS
                    for q in range(2):
                        products(q, nl()[0], GS[q], staged_s[q], (stage_in_s[q], i * 112 + 112))
                    for q in range(2):
                        transposes(q, nl()[0], GS[q])
                    for q in range(2):
                        pe.wait_ge(kdec_r, nl()[0] * 2 + (q + 1))
                        pe.wait_ge(kq_k[q], i + 1)
                        pe.wait_ge(qd_r[q], nl()[0] + 1)
                        for h in range(4):
                            for b in range(NB):
                                last = pe.matmul(kq_bank(q)[:, h, b, :, :], Ss[q][:, h, b, :], kq[q][:, h, b, :, :],
                                                 start=True, stop=True)
                        last.then_inc(kq_ps, 1)
                    for q in range(2):
                        pe.wait_ge(ks_c, i * 2 + (q + 1))
                        pe.wait_ge(vb_r, nl()[0] * 2 + (q + 1))
                        for h in range(4):
                            last = pe.transpose(banks[q][3][0:NR, heads(None, P, h)], kqS[q][:, 0, h, :], ident)
                        last.then_inc(ks_ps[q], 1)
                    for q in range(2):
                        level_y(q, nl(), GS[q], 0)
                    for q in range(2):
                        level_ut(q, nl(), GS[q], 0)
                    for q in range(2):
                        new_values(q, nl(), GS[q])
                    for q in range(2):
                        g, b0 = GS[q], banks[q][0]
                        pe.wait_ge(vn_c[q], nl()[0] + 1)
                        pe.matmul(b0[:, 0:4 * NR], ident, kqS[q][:, 1, :, :].rearrange("p h t -> p (h t)"), start=True, stop=False)
                        for h in range(4):
                            last = pe.matmul(b0[:, heads(g, NR, h)], g.vn[0:NR, h, :], g.attT[0:NR, h, :], start=False, stop=(h == 3))
                        last.then_inc(o_ps[q], 1)
                    for q in range(2):
                        pe.wait_ge(vnm_r[q], i + 1)
                        for h in range(4):
                            for b in range(2):
                                j = 8 * q + 2 * h + b
                                pe.wait_ge(sn_s, i * 16 + (j + 1))
                                pe.matmul(banks[q][1 + 2 * b][:, :], GS[q].kdec[0:NR, h, :],
                                          vnm[q][:, h, 4 * b:4 * b + 4, :].rearrange("p b v -> p (b v)"), start=True, stop=True)\
                                  .then_inc(ds_s, 1)
                pe.wait_ge(group_done[0], 2 * CHUNKS + 4)
                pe.wait_ge(group_done[1], 2 * CHUNKS + 4)
                for q in range(2):
                    pe.wait_ge(o_c[q], 2 * CHUNKS + 3)
                for j in range(HV // HQ):
                    pe.wait_ge(on_sq, j + 1)
                    if j > 0:
                        pe.wait_ge(on_ln, j)
                    for h in range(HQ):
                        for hf in range(2):
                            last = pe.matmul(norm_bank(h, hf), ones_mean, y[:, h, cols(hf)], start=True, stop=True)
                    last.then_inc(on_ms, 1)
                pe.wait_ge(on_ln, HV // HQ)
                with pe.Fori(0, KT) as i:
                    for k in range(2):
                        unit(OUT_BASE + k, i, KT, ohi, olo, k0=KT * k, half_ready=lambda hf: (o_lo, (k + 1) * KT // HQ))
                post(4)

            def delta_in():
                pe.wait_ge(conv_in, 64)
                pe.transpose(aux[2][:, 0:P], convrows[:], ident).then_inc(aux_done, 1)
                for b in range(2):
                    if b:
                        pe.wait_ge(aux_taken, AUX_DN + 1)
                    for k in range(CT // 2):
                        n = NB * (CW - 1)
                        ft = b * CT // 2 + k
                        last = pe.transpose(aux[3 - b][:, k * n:(k + 1) * n], crow[0:n, ft * P:(ft + 1) * P], ident[0:n, 0:n])
                    last.then_inc(aux_done, 1)
                pre(4)
                pe.wait_ge(aux_taken, AUX_DN + 3)
                pe.sem_inc(nq_ms, 2)
                ready = lambda hf: (h_lo, 16 * NTH[4] + 8 * (hf + 1))
                with pe.Fori(0, CT // 2) as i:
                    for k in range(2):
                        unit(IN_BASE + k, i, KT, hhi, hlo, half_ready=ready)
                with pe.Fori(0, ZT // 2) as i:
                    for k in range(2):
                        unit(IN_BASE + CT + k, i, KT, hhi, hlo, half_ready=ready)
                        pe.wait_ge(nq_sq, i * 2 + (k + 1))
                        pe.wait_ge(nq_ln, i * 2 + (k + 1))
                        for hf in range(2):
                            pe.matmul(aux[2 + hf][:, 0:HT], ones_mean, sqn[:, cols(hf)], start=True, stop=True).then_inc(nq_ms, 1)
                unit(OUT_BASE - 1, 0, KT, hhi, hlo, width=2 * HV, half_ready=ready)
                pe.wait_ge(ba_ready, 2)
                pe.wait_ge(nq_ln, 2 * HK + 1)
                for t, n in TT:
                    last = pe.transpose(aux[2][0:n, t * 2 * HV:(t + 1) * 2 * HV], ba[:, t * P:t * P + n], ident[0:2 * HV, 0:2 * HV])
                last.then_inc(aux_done, 1)
                pe.wait_ge(silu_done[1], CT // 2 + 1)
                for b in range(8):
                    pe.wait_ge(aux_taken, AUX_DN + 3 + b)
                    for k in range(4):
                        last = pe.transpose(aux[3 - b % 2][0:CTAIL, k * P:(k + 1) * P], tailc[:, 4 * b + k, :], ident)
                    last.then_inc(aux_done, 1)
                pe.wait_ge(g_step, 7)
                gate = gates[:, G, 0:CHUNKS, :]
                gate_s = gates[0:32, G, CHUNKS, :]
                pe.matmul(aux[0][:, 0:64], upto, gate, start=True, stop=True)
                pe.matmul(aux[0][0:32, 64:80], upto4, gate_s, start=True, stop=True)
                pe.matmul(aux[0][:, 80:144], ones, gate, start=True, stop=True)
                pe.matmul(aux[0][0:32, 144:160], same4, gate_s, start=True, stop=True).then_inc(g_sum, 1)

            pre(0)
            ffn(0, 0)
            post(0)
            pool_mixer()
            for r in (2, 3):
                pre(r)
                ffn(FFN_OF[r], r)
                post(r)
            delta_in()
            delta_core()
            pre(5)
            ffn(3, 5)
            post(5)
            pe.wait_ge(x_ready, 2 * SUBLAYERS + 2)
            pe.wait_ge(aux_taken, AUX_END)
            for t, n in TT:
                for kk in range(2):
                    b = 2 * t + kk
                    if b >= 2:
                        pe.wait_ge(out_copied, b - 1)
                    for k in range(4):
                        last = pe.transpose(aux[2 + b % 2][0:n, k * P:(k + 1) * P], x[:, 4 * kk + k, t * P:t * P + n], ident)
                    last.then_inc(aux_done, 1)

        @block.scalar
        def _(act):
            def root(n, hf):
                act.wait_ge(ms_done, n + 1)
                act.activation(rt[:, hf, :], aux[hf][:, 0:HT], ACT.Sqrt, bias=eps[:]).then_inc(rt_done, 1)

            def pre(r):
                layer, i = r // 3, 2 * (r % 3)
                for hf in range(2):
                    act.wait_ge(x_ready, 2 * r + hf + 1)
                    act.activation(y[:, :, cols(hf)], x[:, :, cols(hf)], ACT.Square).then_inc(x_sq, 1)
                    if r != 1:
                        for k in range(KT):
                            act.activation(hhi[:, k, cols(hf)], x[:, k, cols(hf)], ACT.Copy, scale=gain(layer, i, k))\
                               .then_inc(h_hi, 1)
                for hf in range(2):
                    root(4 * r + hf, hf)

            def post(r):
                for hf in range(2):
                    root(4 * r + 2 + hf, hf)

            def round_weights(unit, i=0):
                s, v = slot(unit), visit(unit)
                nk, width = unit_shape(unit)
                act.wait_ge(raw_full[s], (i + (v + 1)) * 16)
                if v > 0:
                    act.wait_ge(acc_done[s], (i + v) * 2)
                act.activation(whi[s][:, 0:nk, 0:width], wraw[s][:, 0:nk, 0:width], ACT.Copy).then_inc(w_hi[s], 1)

            def next_unit(u, i, n):
                if isinstance(i, int):
                    if u + 2 * n < last_unit:
                        round_weights(u + 2 * n)
                else:
                    round_weights(u + 2, i)

            def steps(n, body):
                with act.Fori(0, n - 1) as i:
                    body(i)
                body(n - 1)

            def square_tile(ready, value, tile, hf, n):
                act.wait_ge(ready, value)
                act.wait_ge(ss_acc, n)
                act.activation(sqt[:, hf:hf + 1, :], y[:, tile, cols(hf)], ACT.Square).then_inc(y_sq, 1)

            def ffn(e, r):
                for f in range(2):
                    base = FFN_BASE[e] + f * (FFN_UNITS // 2)
                    g0 = (2 * e + f) * MF
                    sg, vg = slot(base), visit(base)
                    if (e, f) != (0, 0):
                        last_down = (FFN_BASE[e] if f else FFN_BASE[e - 1] + FFN_UNITS // 2) + FFN_UNITS // 2 - 1
                        act.wait_ge(acc_done[slot(last_down)], 2 * visit(last_down) + 2)

                    def gate_up(i):
                        for hf in range(2):
                            act.wait_ge(taken[sg], (i + vg) * 2 + hf + 3)
                            act.wait_ge(hid_ready, (i + g0) * 2 + 1)
                            act.activation(sil[:, hf, :], tmpg[:, hf, :], ACT.Silu).then_inc(gate_silu, 1)
                        next_unit(base, i, MF)
                        for hf in range(2):
                            act.wait_ge(hid_ready, (i + g0) * 2 + hf + 2)
                            act.activation(hidhi[:, bass.ds(i, 1), cols(hf)], hidf[:, hf:hf + 1, :], ACT.Copy).then_inc(hid_hi, 1)
                        next_unit(base + 1, i, MF)

                    def down(i):
                        for k in range(2):
                            u = base + 2 * MF + k
                            for hf in range(2):
                                if f == 1:
                                    square_tile(taken[slot(u)], (i + visit(u)) * 2 + hf + 3, bass.ds(i * 2 + k, 1), hf,
                                                i * 4 + 16 * r + 2 * k + 1)
                            next_unit(u, i, KT // 2)

                    steps(MF, gate_up)
                    steps(KT // 2, down)

            round_weights(0)
            round_weights(1)
            def delta_in():
                pre(4)
                act.sem_inc(nq_ln, 1)
                act.sem_inc(nq_rs, 1)
                for s in range(2):
                    act.sem_inc(silu_done[s], 1)

                def first_tap(i, k, first, n):
                    u = IN_BASE + first + k
                    s = slot(u)
                    it = i + first // 2
                    ft = bass.ds(i * 2 + (first + k), 1)
                    samp = ub[s][:, CW - 1 + SEQ:UB].rearrange("p (o b t) -> p o b t", o=1, b=NB)
                    act.wait_ge(taken[s], (i + visit(u)) * 2 + 4)
                    act.activation(tailc[:, ft, 0:CW - 1], ub[s][:, SEQ:SEQ + CW - 1].unsqueeze(1), ACT.Copy)
                    act.activation(tailc[:, ft, CW - 1:CTAIL].rearrange("p o (b t) -> p o b t", b=NB),
                                   samp[:, :, :, CW - 1:CW - 1 + NS], ACT.Copy)
                    act.wait_ge(silu_done[s], it + 1)
                    act.activation(conv[s][:, 0:UB - 3], ub[s][:, 0:UB - 3], ACT.Copy, scale=convw[:, ft]).then_inc(tap0[s], 1)
                    next_unit(u, i, n)

                def conv_silu(i, k, first, out, store):
                    s = slot(IN_BASE + first + k)
                    it = i + first // 2
                    act.wait_ge(conv_done[s], it * 3 + 6)
                    if store is not None:
                        act.wait_ge(zv_stored[s], (i + 1) * 16)
                    act.activation(out[:, :, 0:SEQ], conv[s][:, 0:SEQ].unsqueeze(1), ACT.Silu)
                    csamp = conv[s][:, CW - 1 + SEQ:UB].rearrange("p (o b t) -> p o b t", o=1, b=NB)
                    act.activation(out[:, :, SEQ:T].rearrange("p o (b t) -> p o b t", b=NB), csamp[:, :, :, 0:NS], ACT.Silu)\
                       .then_inc(silu_done[s], 1)
                    if store is not None:
                        act.wait_ge(silu_done[s], it + 2)
                        act.dma_start(store, out).then_inc(zv_stored[s], 16)

                for s in range(2):
                    act.sem_inc(zv_stored[s], 16)
                act.wait_ge(conv_pads, 2)
                with act.Fori(0, HK) as i:
                    for k in range(2):
                        first_tap(i, k, 0, HK)
                    for k in range(2):
                        conv_silu(i, k, 0, qk[:, bass.ds(i * 2 + k, 1), :], None)
                with act.Fori(0, HK) as i:
                    for k in range(2):
                        first_tap(i, k, 2 * HK, HK)
                    for k in range(2):
                        conv_silu(i, k, 2 * HK, zv[k][:, :].unsqueeze(1),
                                  v_d[bass.ds(i * 2 + k, 1), :, :].rearrange("o p t -> p o t"))

                def z_tile(i, k, n):
                    u = IN_BASE + CT + k
                    s = slot(u)
                    t = i * 2 + k
                    act.wait_ge(nq_ms, i * 4 + (2 * k + 2))
                    act.activation(sqn[:, :].unsqueeze(1), qk[:, bass.ds(t, 1), :], ACT.Square).then_inc(nq_sq, 1)
                    act.wait_ge(nq_ms, i * 4 + (2 * k + 4))
                    for hf in range(2):
                        last = act.activation(lnn[:, cols(hf)], aux[2 + hf][:, 0:HT], ACT.Ln, bias=eps[:], scale=float(D))
                    last.then_inc(nq_ln, 1)
                    act.wait_ge(nq_ln, t + 2)
                    act.wait_ge(nq_done, t + 1)
                    act.activation(rsn[:, :], lnn[:, :], ACT.Exp, scale=-0.5).then_inc(nq_rs, 1)
                    next_unit(u, i, n)
                    act.wait_ge(taken[s], (i + visit(u)) * 2 + 4)
                    act.dma_start(z_d[bass.ds(t, 1), :, :].rearrange("o p t -> p o t"), zv[k][:, :].unsqueeze(1))\
                       .then_inc(zv_stored[k], 16)
                    act.wait_ge(nq_done, t + 2)
                    act.dma_start(qk_d[bass.ds(t, 1), :, :].rearrange("o p t -> p o t"), qk[:, bass.ds(t, 1), :])\
                       .then_inc(qk_stored, 16)

                def z_pair(i):
                    for k in range(2):
                        z_tile(i, k, ZT // 2)

                steps(ZT // 2, z_pair)
                round_weights(OUT_BASE + 1)
                b, a = bat[:, :, 0:HV], bat[:, :, HV:2 * HV]
                act.wait_ge(g_step, 3)
                act.activation(gtmp[:, 0], b, ACT.Exp, scale=-1.0).then_inc(g_act, 1)
                act.activation(gtmp[:, 2], gtmp[:, 1], ACT.Exp, scale=-1.0).then_inc(g_act, 1)
                act.wait_ge(g_act, 2)
                act.activation(gtmp[:, 3], gtmp[:, 2], ACT.Ln, bias=1.0).then_inc(g_act, 1)
                act.activation(gtmp[:, 7, 0, :], alog[:], ACT.Exp).then_inc(g_act, 1)
                act.wait_ge(g_step, 9)
                act.activation(gates[:, KDEC], gtmp[:, 5], ACT.Exp).then_inc(g_act, 1)
                act.activation(gtmp[:, 6], gates[:, GC], ACT.Exp).then_inc(g_act, 1)

            def flat(a):
                return a.rearrange("p h i -> p (h i)")

            def decays(q, n, g):
                r = g.rows
                act.wait_ge(gate_in[q], n + 1)
                act.wait_ge(dec_sub, n * 2 + (q + 1))
                act.activation(flat(g.eg[:, :, :]), banks[q][1][:, 0:4 * r], ACT.Exp).then_inc(eg_exp, 1)

            def decay_matrix(q, n, g):
                act.wait_ge(dec_sub, n * 2 + (q + 1))
                act.activation(g.dec[0:g.rows], g.dec[0:g.rows], ACT.Exp, scale=-1.0).then_inc(dec_exp, 1)

            def copies(q, n, g):
                r = g.rows
                act.wait_ge(tr_ps[q], n * 2 + 1)
                act.activation(flat(g.attT[0:r]), banks[q][1][0:r, 0:4 * r], ACT.Copy).then_inc(att_c, 1)
                act.wait_ge(tr_ps[q], n * 2 + 2)
                act.activation(flat(g.U[0:r]), banks[q][0][0:r, 0:4 * r], ACT.Copy).then_inc(u_c, 1)

            def values(q, n, g):
                r = g.rows
                act.wait_ge(vn_ps[q], n + 1)
                act.activation(flat(g.vn[0:r]), banks[q][3][0:r, :], ACT.Copy).then_inc(vn_c[q], 1)

            def outputs(q, n, g, dst):
                r = g.rows
                act.wait_ge(o_ps[q], n + 1)
                act.wait_ge(o_stored[q], n * 16 + 16)
                act.activation(flat(g.oT[:, :, :]), banks[q][0][:, 0:4 * r], ACT.Copy).then_inc(o_c[q], 1)
                act.wait_ge(o_c[q], n + 2)
                act.dma_start(dst.rearrange("h p t -> p h t"), g.oT[:, :, :]).then_inc(o_stored[q], 16)

            def delta_core():
                for q in range(2):
                    act.sem_inc(o_c[q], 1)
                    act.sem_inc(o_stored[q], 16)
                with act.Fori(0, CHUNKS) as i:
                    for p in range(2):
                        for q in range(2):
                            decay_matrix(q, i * 2 + p, GP[q])
                            decays(q, i * 2 + p, GP[q])
                        for q in range(2):
                            copies(q, i * 2 + p, GP[q])
                        for q in range(2):
                            values(q, i * 2 + p, GP[q])
                        for q in range(2):
                            g = 2 * p + q
                            outputs(q, i * 2 + p, GP[q], o_d[4 * g:4 * g + 4, :, bass.ds(i * P, P)])
                act.wait_ge(sample_go, 1)
                with act.Fori(0, 2) as i:
                    n = i + 2 * CHUNKS
                    for stage in (decay_matrix, decays, copies):
                        for q in range(2):
                            stage(q, i + 2 * CHUNKS, GS[q])
                    for q in range(2):
                        act.wait_ge(kq_ps, i * 2 + (q + 1))
                        for z in range(2):
                            last = act.activation(kqS[q][:, z, :, :].rearrange("p h (b t) -> p h b t", b=NB), kq_bank(q)[:, :, :, z, :],
                                                  ACT.Copy)
                        last.then_inc(ks_c, 1)
                    for q in range(2):
                        values(q, i + 2 * CHUNKS, GS[q])
                    for q in range(2):
                        outputs(q, i + 2 * CHUNKS, GS[q], o_d[bass.ds(i * 8 + 4 * q, 4), :, SEQ:T])
                def gate(j):
                    act.wait_ge(of_in[j % 2], 32 * (j // 2 + 1))
                    act.activation(zs[j % 2][:, :, :], zs[j % 2][:, :, :], ACT.Silu).then_inc(z_silu, 1)

                gate(0)
                for j in range(HV // HQ):
                    act.wait_ge(on_ms, j + 1)
                    if j > 0:
                        act.wait_ge(on_norm, j)
                    for h in range(2):
                        act.activation(y[:, HQ + h, :].rearrange("p (f t) -> p f t", f=2), acc[h][:, :, 0:HT], ACT.Ln,
                                       bias=eps[:], scale=float(KT))
                    for h in range(2, HQ):
                        for hf in range(2):
                            last = act.activation(y[:, HQ + h, cols(hf)], norm_bank(h, hf), ACT.Ln, bias=eps[:], scale=float(KT))
                    last.then_inc(on_ln, 1)
                    act.wait_ge(on_ln, j + 1)
                    act.activation(y[:, HQ:2 * HQ, :], y[:, HQ:2 * HQ, :], ACT.Exp, scale=-0.5).then_inc(on_rs, 1)
                    if j + 1 < HV // HQ:
                        gate(j + 1)
                    act.wait_ge(on_gate, j + 1)
                    act.activation(ohi[:, HQ * j:HQ * (j + 1), :], of[j % 2][:, :, :], ACT.Copy).then_inc(o_hi, 1)

                def out_tile(i):
                    for k in range(2):
                        u = OUT_BASE + k
                        if k == 1:
                            for hf in range(2):
                                square_tile(taken[slot(u)], (i + visit(u)) * 2 + hf + 3, bass.ds(i, 1), hf, i * 2 + 65)
                        else:
                            act.wait_ge(acc_done[slot(u)], (i + visit(u)) * 2 + 2)
                        next_unit(u, i, KT)

                steps(KT, out_tile)
                post(4)

            act.sem_inc(gate_silu, 1)
            act.wait_ge(setup_done, 1)

            def pool_mixer():
                pre(1)
                for mt in range(KT):
                    for hf in range(2):
                        square_tile(pool_y, 2 * mt + hf + 1, slice(mt, mt + 1), hf, 16 + 2 * mt + 1)
                post(1)
                act.dma_start(O["pool_sample"][0, :, 0:POOLP - NS, :], I["state_pool"][0, :, NS:POOLP, :]).then_inc(pool_stored, 16)
                act.wait_ge(aux_taken, AUX_TAIL + 2)
                act.dma_start(O["pool_prompt"][0, 0, :, :], tailrows[0:POOLP, :]).then_inc(pool_stored, 16)
                for b in range(NB):
                    act.dma_start(O["pool_sample"][0, b, POOLP - NS:POOLP, :],
                                  tailrows[POOLP + NS * b:POOLP + NS * (b + 1), :]).then_inc(pool_stored, 16)
                act.wait_ge(pool_stored, 16 * (NB + 2))

            pre(0)
            ffn(0, 0)
            post(0)
            pool_mixer()
            for r in (2, 3):
                pre(r)
                ffn(FFN_OF[r], r)
                post(r)
            delta_in()
            delta_core()
            pre(5)
            ffn(3, 5)
            post(5)

        @block.vector
        def _(dve):
            def take(u, i, hf):
                s, v = slot(u), visit(u)
                dve.wait_ge(acc_done[s], (i + v) * 2 + hf + 1)
                return acc[s][:, hf, 0:HT]

            def reciprocal(n, hf, dst):
                dve.wait_ge(rt_done, n + 1)
                dve.reciprocal(dst[:, hf, :], rt[:, hf, :]).then_inc(rb_ready, 1)

            def pre(r):
                layer, i = r // 3, 2 * (r % 3)
                for hf in range(2):
                    for k in range(KT if r != 1 else 0):
                        dve.wait_ge(h_hi, 16 * NTH[r] + 8 * hf + k + 1)
                        dve.scalar_tensor_tensor(hlo[:, k, cols(hf)], x[:, k, cols(hf)], gain(layer, i, k),
                                                 hhi[:, k, cols(hf)].bitcast(F), ALU.mult, ALU.subtract).then_inc(h_lo, 1)
                for hf in range(2):
                    reciprocal(4 * r + hf, hf, rpre)

            def post(r):
                if r in (1, 4):
                    g = lambda k: gain(r // 3, 3, k)
                else:
                    g = lambda k: gpost[:, FFN_OF[r], k:k + 1]
                for hf in range(2):
                    reciprocal(4 * r + 2 + hf, hf, rpost)
                    dve.wait_ge(rb_ready, 4 * r + 2 + hf + 1)
                    for k in range(KT):
                        dve.scalar_tensor_tensor(y[:, k, cols(hf)], y[:, k, cols(hf)], g(k), rpost[:, hf, :],
                                                 ALU.mult, ALU.mult).then_inc(y_norm, 1)
                    dve.wait_ge(y_norm, 16 * r + 8 * (hf + 1))
                    dve.tensor_tensor(x[:, :, cols(hf)], x[:, :, cols(hf)], y[:, :, cols(hf)], ALU.add).then_inc(x_ready, 1)

            def ffn(e, r):
                for f in range(2):
                    base = FFN_BASE[e] + f * (FFN_UNITS // 2)
                    g0 = (2 * e + f) * MF
                    sg, su = slot(base), slot(base + 1)
                    vg, vu = visit(base), visit(base + 1)
                    if f == 0:
                        dve.wait_ge(rb_ready, 4 * r + 2)
                    with dve.Fori(0, MF) as i:
                        dve.wait_ge(gate_silu, (i + g0) * 2 + 1)
                        for hf in range(2):
                            dve.tensor_tensor(tmpg[:, hf, :], take(base, i, hf), rpre[:, hf, :], ALU.mult).then_inc(taken[sg], 1)
                        for hf in range(2):
                            dve.tensor_tensor(tmpu[:, hf, :], take(base + 1, i, hf), rpre[:, hf, :], ALU.mult)\
                               .then_inc(taken[su], 1)
                            dve.wait_ge(gate_silu, (i + g0) * 2 + hf + 2)
                            dve.wait_ge(taken[su], (i + vu) * 2 + hf + 3)
                            dve.tensor_tensor(hidf[:, hf, :], tmpu[:, hf, :], sil[:, hf, :], ALU.mult).then_inc(hid_ready, 1)
                        for hf in range(2):
                            dve.wait_ge(hid_hi, (i + g0) * 2 + hf + 1)
                            dve.tensor_tensor(hidlo[:, bass.ds(i, 1), cols(hf)], hidf[:, hf:hf + 1, :],
                                              hidhi[:, bass.ds(i, 1), cols(hf)].bitcast(F), ALU.subtract).then_inc(hid_lo, 1)
                    if f == 1:
                        dve.memset(ssacc[:], 0.0).then_inc(ss_zero, 1)
                        dve.wait_ge(ss_zero, r + 1)
                    with dve.Fori(0, KT // 2) as i:
                        for k in range(2):
                            u = base + 2 * MF + k
                            yt = lambda hf: y[:, bass.ds(i * 2 + k, 1), cols(hf)]
                            for hf in range(2):
                                src = take(u, i, hf).rearrange("p (o n) -> p o n", o=1)
                                if f == 0:
                                    dve.tensor_copy(yt(hf), src).then_inc(taken[slot(u)], 1)
                                else:
                                    dve.tensor_tensor(yt(hf), src, yt(hf), ALU.add).then_inc(taken[slot(u)], 1)
                            if f == 1:
                                for hf in range(2):
                                    dve.wait_ge(y_sq, i * 4 + 16 * r + 2 * k + hf + 1)
                                    dve.wait_ge(ss_acc, i * 4 + 16 * r + 2 * k + 1)
                                    dve.tensor_tensor(ssacc[:, hf, :], ssacc[:, hf, :], sqt[:, hf, :], ALU.add).then_inc(ss_acc, 1)

            for s in range(2):
                dve.sem_inc(taken[s], 2)
            dve.sem_inc(hid_ready, 1)
            dve.sem_inc(ss_acc, 1)
            dve.memset(eps[:], EPS)
            dve.memset(ssacc[:], 0.0)
            dve.wait_ge(aux_done, 1)
            dve.tensor_copy(gains[:, 0:105], aux[3][:, 0:105]).then_inc(aux_taken, 1)
            dve.wait_ge(aux_taken, 1)
            gg = gains[:, 0:96].rearrange("p (l j i k) -> p l j i k", l=2, j=3, i=2)
            for l in range(2):
                for j in range(2):
                    last = dve.tensor_scalar(gpost[:, 2 * l + j, :], gg[:, l, 2 * j, 1, :], 0.5, None, ALU.mult)
            last.then_inc(setup_done, 1)
            dve.wait_ge(setup_done, 1)
            for t, n in TT:
                for kk in range(2):
                    b = 2 * t + kk
                    dve.wait_ge(aux_done, b + 2)
                    c = dve.tensor_copy(x[:, 4 * kk:4 * kk + 4, t * P:t * P + n],
                                        aux[b % 2][:, 0:4 * n].rearrange("p (k n) -> p k n", k=4)).then_inc(aux_taken, 1)
            dve.wait_ge(aux_taken, 11)
            dve.sem_inc(x_ready, 2)

            def samples(a, pad):
                return a.rearrange("p (b t) -> p b t", b=NB)[:, :, pad:pad + NS]

            def pairs(a):
                n = a.shape[-1] // 2
                return a.rearrange("p (k i) -> p k i", k=2).unsqueeze(2).broadcast_to([a.shape[0], 2, 2, n])

            def by_key(a):
                return a.rearrange("p (k v) i -> p k v i", k=2)

            def gate_of(g, kind, n):
                return g.gate[0:g.rows, kind, :].unsqueeze(2).broadcast_to([g.rows, 4, n])

            def four(bank, r, n):
                return bank[0:r, 0:4 * n].rearrange("p (h i) -> p h i", h=4)

            def copy_gates(q, n, g, src):
                dve.wait_ge(group_done[q], n + 2)
                dve.tensor_copy(g.gate[0:g.rows, :, :].unsqueeze(2), src).then_inc(gate_in[q], 1)

            def decay_start(q, n, g):
                r, (b0, b1, b2, b3) = g.rows, banks[q]
                dve.wait_ge(gate_in[q], n + 1)
                dve.wait_ge(gcb_ps, n * 2 + (q + 1))
                fut = future if r == P else future4
                for h in range(4):
                    last = dve.scalar_tensor_tensor(g.dec[0:r, h, :], b1[0:r, h * r:(h + 1) * r], g.gate[0:r, GC, h:h + 1], fut,
                                                    ALU.subtract, ALU.add)
                last.then_inc(dec_sub, 1)

            def by_token(q, n, g):
                r, (b0, b1, b2, b3) = g.rows, banks[q]
                dve.wait_ge(kv_ps, n * 2 + (q + 1))
                dve.tensor_tensor(by_key(g.kdec[0:r]), pairs(b2[0:r, 0:2 * P]), by_key(gate_of(g, KDEC, P)), ALU.mult)\
                   .then_inc(kdec_r, 1)
                dve.tensor_tensor(g.vb[0:r], four(b3, r, P), gate_of(g, BETA, P), ALU.mult).then_inc(vb_r, 1)

            def decayed(q, n, g):
                r, (b0, b1, b2, b3) = g.rows, banks[q]
                dve.wait_ge(kk_ps, n * 2 + (q + 1))
                dve.wait_ge(dec_exp, n * 2 + (q + 1))
                dve.tensor_tensor(by_key(g.kd[0:r]), pairs(b0[0:r, 0:2 * r]), by_key(g.dec[0:r]), ALU.mult).then_inc(kd_r, 1)
                dve.wait_ge(kd_r, n * 2 + (q + 1))
                dve.wait_ge(beta_r[q], n + 1)
                dve.tensor_tensor(g.low[0:r], g.kd[0:r], g.low[0:r], ALU.mult).then_inc(low_r, 1)

            def lower(n, g):
                r = g.rows
                dve.wait_ge(low_r, n * 2 + 2)
                dve.tensor_tensor(g.kd[0:r], g.low[0:r], minus_pairs[0:r, 0:r].unsqueeze(1).broadcast_to([r, 4, r]), ALU.mult)\
                   .then_inc(t0a[1], 1)
                dve.wait_ge(t0a[1], n + 1)
                dve.tensor_tensor(g.T[0:r], g.kd[0:r], ident[0:r, 0:r].unsqueeze(1).broadcast_to([r, 4, r]), ALU.add)\
                   .then_inc(t0[1], 1)

            def decayed_queries(q, n, g):
                r, b0 = g.rows, banks[q][0]
                dve.tensor_tensor(by_key(g.att[0:r]), pairs(b0[0:r, 2 * r:4 * r]), by_key(g.dec[0:r]), ALU.mult).then_inc(att_r, 1)

            def key_state(q, n, g):
                r, (b0, b1, b2, b3) = g.rows, banks[q]
                dve.wait_ge(ks_ps[q], n + 1)
                dve.tensor_tensor(g.rv[0:r], four(b2 if r == P else b3, r, P), gate_of(g, NBE, P), ALU.mult).then_inc(ks_r[q], 1)

            def halves4(a, lv):
                return a.rearrange("p h (b two l) -> p h b two l", two=2, l=2 << lv)

            def level_y(q, n, nl, g, lv):
                r, (b0, b1, b2, b3) = g.rows, banks[q]
                dve.wait_ge(y_ps[q], nl + lv + 1)
                m = partner[lv][0:r, 0:r // 2].rearrange("p (b l) -> p b l", l=2 << lv)
                dve.tensor_tensor(halves4(g.Y[lv][0:r], lv)[:, :, :, 1, :],
                                  b0[0:r, 0:2 * r].rearrange("p (h b l) -> p h b l", h=4, l=2 << lv),
                                  m.unsqueeze(1).broadcast_to([r, 4, r // (4 << lv), 2 << lv]), ALU.mult).then_inc(y_r[q], 1)

            def level_ut(q, n, nl, g, lv):
                r, (b0, b1, b2, b3) = g.rows, banks[q]
                dve.wait_ge(ut_ps[q], nl + lv + 1)
                bank = b1[0:r, 0:4 * r].rearrange("p (z h b l) -> p z h b l", z=2, h=4, l=2 << lv)
                u = halves4(g.U[0:r], lv)[:, :, :, 1, :]
                last = dve.tensor_tensor(u, u, bank[:, 0], ALU.subtract)
                if lv < g.levels - 1:
                    t = halves4(g.T[0:r], lv)[:, :, :, 0, :]
                    last = dve.tensor_tensor(t, t, bank[:, 1], ALU.subtract)
                last.then_inc(ut_r[q], 1)

            def delta_core():
                dve.wait_ge(qk_stored, 16 * 2 * HK)
                for s in range(2):
                    dve.wait_ge(zv_stored[s], 16 * (HV + 1))
                dve.wait_ge(conv_stored, 16 * (NB + 1))
                for q in range(2):
                    for n in range(LEVELS):
                        dve.memset(GP[q].Y[n][:], 0.0)
                dve.memset(S[:], 0.0)
                for q in range(2):
                    dve.memset(GP[q].gate[:], 0.0).then_inc(group_done[q], 2)
                with dve.Fori(0, CHUNKS) as i:
                    for p in range(2):
                        for q in range(2):
                            g = 2 * p + q
                            copy_gates(q, i * 2 + p, GP[q], gates[:, :, bass.ds(i, 1), 4 * g:4 * g + 4])
                        for q in range(2):
                            decay_start(q, i * 2 + p, GP[q])
                        for q in range(2):
                            decayed(q, i * 2 + p, GP[q])
                        for q in range(2):
                            decayed_queries(q, i * 2 + p, GP[q])
                        lower(i * 2 + p, GP[1])
                        for q in range(2):
                            by_token(q, i * 2 + p, GP[q])
                        for q in range(2):
                            key_state(q, i * 2 + p, GP[q])
                        for lv in range(LEVELS):
                            for q in range(2):
                                level_y(q, i * 2 + p, i * 12 + 6 * p, GP[q], lv)
                            for q in range(2):
                                level_ut(q, i * 2 + p, i * 12 + 6 * p, GP[q], lv)
                        for q in range(2):
                            hs = slice(4 * (2 * p + q), 4 * (2 * p + q) + 4)
                            dve.wait_ge(sd_r[q], i * 2 + (p + 1))
                            dve.wait_ge(ds_ps[q], i * 2 + (p + 1))
                            dve.tensor_tensor(S[:, hs, :], Sd[q][:, :, :], four(banks[q][1], P, P), ALU.add).then_inc(group_done[q], 1)
                dve.wait_ge(sample_go, 1)
                for q in range(2):
                    dve.memset(GS[q].Y[0][:], 0.0)
                dve.memset(GS[0].gate[:], 0.0).then_inc(sn_s, 2)
                dve.wait_ge(sn_s, 2)
                with dve.Fori(0, 2) as i:
                    m, ml = 2 * CHUNKS, 2 * CHUNKS * LEVELS
                    for q in range(2):
                        copy_gates(q, i + m, GS[q], gates[0:NR, :, CHUNKS:CHUNKS + 1, bass.ds(i * 8 + 4 * q, 4)])
                    for q in range(2):
                        dve.wait_ge(stage_in_s[q], i * 112 + 112)
                        for v in range(2):
                            last = dve.tensor_copy(kq[q][:, v::2, :, 0, :], staged_s[q].k[:, :, :].rearrange("p k (b t) -> p k b t", b=NB))
                        last.then_inc(kq_k[q], 1)
                    for q in range(2):
                        decay_start(q, i + m, GS[q])
                    for q in range(2):
                        decayed(q, i + m, GS[q])
                    lower(i + m, GS[1])
                    for q in range(2):
                        by_token(q, i + m, GS[q])
                    for q in range(2):
                        decayed_queries(q, i + m, GS[q])
                    for q in range(2):
                        key_state(q, i + m, GS[q])
                    for q in range(2):
                        level_y(q, i + m, i + ml, GS[q], 0)
                    for q in range(2):
                        level_ut(q, i + m, i + ml, GS[q], 0)
                    for q in range(2):
                        dve.wait_ge(vn_c[q], i + (m + 1))
                        for h in range(4):
                            last = dve.tensor_tensor(vnm[q][:, h, :, :], GS[q].vn[0:NR, h, :].unsqueeze(1).broadcast_to([NR, NB, P]),
                                                     seq_rows.unsqueeze(2).broadcast_to([NR, NB, P]), ALU.mult)
                        last.then_inc(vnm_r[q], 1)
                    for q in range(2):
                        for h in range(4):
                            j = 4 * q + h
                            dve.wait_ge(sd_s, i * 8 + (j + 3))
                            for b in range(2):
                                dve.wait_ge(ds_s, i * 16 + (2 * j + b + 1))
                                c = slice(4 * b, 4 * b + 4)
                                dve.tensor_tensor(Ss[q][:, h, c, :], Sds[h % 2][:, c, :],
                                                  banks[q][1 + 2 * b][:, :].rearrange("p (b v) -> p b v", b=4), ALU.add)\
                                   .then_inc(sn_s, 1)
                        dve.wait_ge(sn_s, i * 16 + (8 * q + 10))
                        dve.sem_inc(group_done[q], 1)
                for j in range(HV // HQ):
                    o, hs = of[j % 2], slice(HQ * j, HQ * (j + 1))
                    dve.wait_ge(on_rs, j + 1)
                    dve.scalar_tensor_tensor(o[:, :, :], o[:, :, :], gains[:, 104:105], y[:, HQ:2 * HQ, :], ALU.mult, ALU.mult)\
                       .then_inc(on_norm, 1)
                    dve.wait_ge(on_norm, j + 1)
                    dve.wait_ge(z_silu, j + 1)
                    dve.tensor_tensor(o[:, :, :], o[:, :, :], zs[j % 2][:, :, :], ALU.mult).then_inc(on_gate, 1)
                    dve.wait_ge(o_hi, j + 1)
                    dve.tensor_tensor(olo[:, hs, :], o[:, :, :], ohi[:, hs, :].bitcast(F), ALU.subtract).then_inc(o_lo, 1)
                dve.memset(ssacc[:], 0.0).then_inc(ss_zero, 1)
                dve.wait_ge(ss_zero, 5)
                with dve.Fori(0, KT) as i:
                    yt = lambda hf: y[:, bass.ds(i, 1), cols(hf)]
                    for k in range(2):
                        u = OUT_BASE + k
                        for hf in range(2):
                            src = take(u, i, hf).unsqueeze(1)
                            if k == 0:
                                dve.tensor_copy(yt(hf), src).then_inc(taken[slot(u)], 1)
                            else:
                                if hf == 0:
                                    dve.wait_ge(taken[slot(u - 1)], (i + visit(u - 1)) * 2 + 4)
                                dve.tensor_tensor(yt(hf), src, yt(hf), ALU.add).then_inc(taken[slot(u)], 1)
                    for hf in range(2):
                        dve.wait_ge(y_sq, i * 2 + (64 + hf + 1))
                        dve.wait_ge(ss_acc, i * 2 + 65)
                        dve.tensor_tensor(ssacc[:, hf, :], ssacc[:, hf, :], sqt[:, hf, :], ALU.add).then_inc(ss_acc, 1)
                post(4)

            def delta_in():
                for s in range(2):
                    dve.sem_inc(conv_done[s], 3)
                dve.sem_inc(nq_done, 1)
                for s in range(2):
                    dve.memset(ub[s][:, 0:CW - 1], 0.0)
                dve.memset(gates[:], 0.0).then_inc(conv_pads, 1)
                dve.memset(bat[:], 0.0)
                dve.wait_ge(aux_done, AUX_DN + 1)
                dve.tensor_copy(convw[:], aux[2][:, 0:P]).then_inc(aux_taken, 1)
                for b in range(2):
                    dve.wait_ge(aux_done, AUX_DN + 2 + b)
                    dve.tensor_copy(pastc[:, b * CT // 2:(b + 1) * CT // 2, :],
                                    aux[3 - b][:, 0:384].rearrange("p (k n) -> p k n", n=NB * (CW - 1))).then_inc(aux_taken, 1)
                dve.wait_ge(aux_taken, AUX_DN + 3)
                dve.sem_inc(conv_pads, 1)
                pre(4)
                dve.wait_ge(rb_ready, 18)
                with dve.Fori(0, CT // 2) as i:
                    for k in range(2):
                        u = IN_BASE + k
                        s = slot(u)
                        samp = ub[s][:, CW - 1 + SEQ:UB].rearrange("p (b t) -> p b t", b=NB)
                        dve.wait_ge(conv_done[s], i * 3 + 3)
                        dve.tensor_copy(samp[:, :, 0:CW - 1].unsqueeze(1),
                                        pastc[:, bass.ds(i * 2 + k, 1), :].rearrange("p o (b t) -> p o b t", b=NB))
                        dve.tensor_tensor(ub[s][:, CW - 1:CW - 1 + HT], take(u, i, 0), rpre[:, 0, :], ALU.mult).then_inc(taken[s], 1)
                        bank = take(u, i, 1)
                        n = SEQ - HT
                        dve.tensor_tensor(ub[s][:, CW - 1 + HT:CW - 1 + SEQ], bank[:, 0:n], rpre[:, 1, 0:n], ALU.mult)
                        dve.tensor_tensor(samp[:, :, CW - 1:CW - 1 + NS], samples(bank[:, n:HT], 0), samples(rpre[:, 1, n:HT], 0),
                                          ALU.mult).then_inc(taken[s], 1)
                        dve.wait_ge(taken[s], (i + visit(u)) * 2 + 4)
                        for j in range(1, CW):
                            if j == 1:
                                dve.wait_ge(tap0[s], i + 1)
                            else:
                                dve.wait_ge(conv_done[s], i * 3 + (j + 2))
                            w = convw[:, bass.ds(i * 2 + (32 * j + k), 1)]
                            dve.scalar_tensor_tensor(conv[s][:, 0:UB - 3], ub[s][:, j:UB - 3 + j], w, conv[s][:, 0:UB - 3],
                                                     ALU.mult, ALU.add).then_inc(conv_done[s], 1)
                for part, c in ((0, float(DK) ** -0.5), (1, 1.0)):
                    with dve.Fori(0, HK // 2) as i:
                        for k in range(2):
                            u = IN_BASE + CT + HK * part + k
                            m = i + (HK // 2 * part + HK)
                            dve.wait_ge(zv_stored[k], (m + 1) * 16)
                            for hf in range(2):
                                dve.tensor_tensor(zv[k][:, cols(hf)], take(u, i, hf), rpre[:, hf, :], ALU.mult)\
                                   .then_inc(taken[slot(u)], 1)
                            t = i * 2 + (HK * part + k)
                            dve.wait_ge(nq_rs, t + 2)
                            tile = qk[:, bass.ds(t, 1), :]
                            dve.scalar_tensor_tensor(tile, tile, c, rsn[:, :].unsqueeze(1), ALU.mult, ALU.mult).then_inc(nq_done, 1)
                u = OUT_BASE - 1
                for hf in range(2):
                    bank = take(u, 0, hf)
                    dve.tensor_tensor(ba[:, cols(hf)], bank[0:2 * HV, :], rpre[0:2 * HV, hf, :], ALU.mult).then_inc(taken[slot(u)], 1)
                dve.wait_ge(taken[slot(u)], 2 * visit(u) + 4)
                dve.sem_inc(ba_ready, 2)
                dve.wait_ge(aux_done, AUX_DN + 4)
                dve.tensor_copy(bat[:, 0:CHUNKS, :], aux[2][:, 0:CHUNKS * 2 * HV].rearrange("p (c n) -> p c n", c=CHUNKS))
                dve.tensor_copy(bat[0:32, CHUNKS, :], aux[2][0:32, CHUNKS * 2 * HV:(CHUNKS + 1) * 2 * HV]).then_inc(aux_taken, 1)
                dve.wait_ge(aux_taken, AUX_DN + 4)
                b, a = bat[:, :, 0:HV], bat[:, :, HV:2 * HV]
                dt = dtb[:, :].unsqueeze(1).broadcast_to([P, CHUNKS + 1, HV])
                dve.tensor_tensor(a, a, dt, ALU.add).then_inc(g_step, 1)
                dve.wait_ge(g_step, 1)
                dve.tensor_scalar(gtmp[:, 0], a, -1.0, None, ALU.mult).then_inc(g_step, 1)
                dve.wait_ge(g_step, 2)
                dve.tensor_tensor(gtmp[:, 1], gtmp[:, 0], a, ALU.max).then_inc(g_step, 1)
                dve.wait_ge(g_act, 4)
                dve.tensor_scalar(gtmp[:, 0], gtmp[:, 0], 1.0, None, ALU.add).then_inc(g_step, 1)
                dve.wait_ge(g_step, 4)
                dve.reciprocal(gates[:, BETA], gtmp[:, 0]).then_inc(g_step, 1)
                dve.scalar_tensor_tensor(gtmp[:, 4], a, 0.0, gtmp[:, 3], ALU.max, ALU.add).then_inc(g_step, 1)
                dve.wait_ge(g_step, 6)
                for c in range(CHUNKS + 1):
                    n = P if c < CHUNKS else 32
                    last = dve.scalar_tensor_tensor(gates[0:n, G, c, :], gtmp[0:n, 4, c, :], -1.0, gtmp[0:n, 7, 0, :],
                                                    ALU.mult, ALU.mult)
                last.then_inc(g_step, 1)
                for bb in range(8):
                    dve.wait_ge(aux_done, AUX_DN + 5 + bb)
                    dve.tensor_copy(crow[:, bb * 512:(bb + 1) * 512], aux[3 - bb % 2][0:CTAIL, :]).then_inc(aux_taken, 1)
                dve.wait_ge(g_sum, 1)
                dve.memset(gtmp[:, 5], 0.0).then_inc(g_step, 1)
                dve.wait_ge(g_step, 8)
                dve.tensor_copy(gates[:, GC, 0:CHUNKS, :], aux[0][:, 0:64].rearrange("p (c h) -> p c h", c=CHUNKS))
                dve.tensor_copy(gates[0:32, GC, CHUNKS, :], aux[0][0:32, 64:80]).then_inc(gates_ready, 1)
                dve.wait_ge(gates_ready, 1)
                dve.tensor_tensor(gtmp[:, 5, 0:CHUNKS, :], aux[0][:, 80:144].rearrange("p (c h) -> p c h", c=CHUNKS),
                                  gates[:, GC, 0:CHUNKS, :], ALU.subtract)
                dve.tensor_tensor(gtmp[0:32, 5, CHUNKS, :], aux[0][0:32, 144:160], gates[0:32, GC, CHUNKS, :],
                                  ALU.subtract).then_inc(g_step, 1)
                dve.wait_ge(g_act, 6)
                dve.scalar_tensor_tensor(gates[:, NBE], gtmp[:, 6], -1.0, gates[:, BETA], ALU.mult, ALU.mult).then_inc(gates_ready, 1)

            def pool_mixer():
                dve.memset(hp[:, :, 0:POOLP], 0.0).then_inc(hp_ready, 1)
                for b in range(2):
                    dve.wait_ge(aux_done, AUX_PAST + b + 1)
                    dst = hp[:, 4 * b:4 * b + 4, POOLP + SEQ:HP].rearrange("p k (b t) -> p k b t", b=NB)[:, :, :, 0:POOLP]
                    dve.tensor_copy(dst, aux[2 + b][:, 0:480].rearrange("p (k b t) -> p k b t", k=4, b=NB)).then_inc(aux_taken, 1)
                pre(1)
                dve.wait_ge(rb_ready, 6)
                for k in range(KT):
                    g = gain(0, 2, k)
                    dve.scalar_tensor_tensor(hp[:, k, POOLP:POOLP + HT], x[:, k, 0:HT], g, rpre[:, 0, :], ALU.mult, ALU.mult)
                    dve.scalar_tensor_tensor(hp[:, k, POOLP + HT:POOLP + SEQ], x[:, k, HT:SEQ], g, rpre[:, 1, 0:SEQ - HT],
                                             ALU.mult, ALU.mult)
                    dve.scalar_tensor_tensor(samples(hp[:, k, POOLP + SEQ:HP], POOLP), samples(x[:, k, SEQ:T], 0), g,
                                             samples(rpre[:, 1, SEQ - HT:HT], 0), ALU.mult, ALU.mult).then_inc(hp_ready, 1)
                dve.wait_ge(hp_ready, KT + 1)
                dve.tensor_copy(tail[:, :, 0:POOLP], hp[:, :, SEQ:SEQ + POOLP]).then_inc(tail_ready, 1)
                dve.tensor_copy(tail[:, :, POOLP:HTAIL].rearrange("p k (b t) -> p k b t", b=NB),
                                hp[:, :, POOLP + SEQ:HP].rearrange("p k (b t) -> p k b t", b=NB)[:, :, :, POOLP:POOLP + NS])\
                   .then_inc(tail_ready, 1)
                dve.sem_inc(hp_ready, 2)
                n = 0
                for g, w in enumerate(WINDOWS):
                    two = slice(2 * g, 2 * g + 2)
                    src = hp[:, two, :]
                    if g < 3:
                        for j in range(g + 1):
                            h, dst = 1 << j, winv[j % 2]
                            if n:
                                dve.wait_ge(win_dve, n)
                            if j == 0 and g:
                                dve.wait_ge(pooled_ready, g)
                            dve.tensor_tensor(dst[:, :, 2 * h - 1:HP], src[:, :, 2 * h - 1:HP], src[:, :, h - 1:HP - h], ALU.add)\
                               .then_inc(win_dve, 1)
                            n += 1
                            src = dst
                    else:
                        dve.wait_ge(win_pool, 4)
                        src = winp[1]
                    dve.wait_ge(win_dve, n)
                    dve.tensor_tensor(src[:, :, POOLP:POOLP + 16], src[:, :, POOLP:POOLP + 16],
                                      fix[:, g:g + 1, :].broadcast_to([P, 2, 16]), ALU.mult).then_inc(win_dve, 1)
                    n += 1
                    dve.wait_ge(win_dve, n)
                    dve.scalar_tensor_tensor(pooled[:, two, 0:SEQ], src[:, :, POOLP:POOLP + SEQ], 1.0 / w,
                                             hp[:, two, POOLP:POOLP + SEQ], ALU.mult, ALU.subtract).then_inc(win_dve, 1)
                    n += 1
                    for k in range(2):
                        last = dve.scalar_tensor_tensor(samples(pooled[:, 2 * g + k, SEQ:T], 0),
                                                        samples(src[:, k, POOLP + SEQ:HP], POOLP), 1.0 / w,
                                                        samples(hp[:, 2 * g + k, POOLP + SEQ:HP], POOLP), ALU.mult, ALU.subtract)
                    last.then_inc(pooled_ready, 1)
                for b in range(2):
                    dve.wait_ge(aux_done, AUX_TAIL + b + 1)
                    dve.tensor_copy(tailrows[:, b * 512:(b + 1) * 512], aux[2 + b][0:HTAIL, :]).then_inc(aux_taken, 1)
                dve.memset(ssacc[:], 0.0).then_inc(ss_zero, 1)
                dve.wait_ge(ss_zero, 2)
                for mt in range(KT):
                    for hf in range(2):
                        dve.wait_ge(pool_mm, 2 * mt + hf + 1)
                        dve.tensor_scalar(y[:, mt, cols(hf)], aux[2 + hf][:, 0:HT], gains[:, 96 + mt:97 + mt], None, ALU.mult)\
                           .then_inc(pool_y, 1)
                    for hf in range(2):
                        dve.wait_ge(y_sq, 16 + 2 * mt + hf + 1)
                        dve.wait_ge(ss_acc, 16 + 2 * mt + 1)
                        dve.tensor_tensor(ssacc[:, hf, :], ssacc[:, hf, :], sqt[:, hf, :], ALU.add).then_inc(ss_acc, 1)
                post(1)

            pre(0)
            ffn(0, 0)
            post(0)
            pool_mixer()
            for r in (2, 3):
                pre(r)
                ffn(FFN_OF[r], r)
                post(r)
            delta_in()
            delta_core()
            pre(5)
            ffn(3, 5)
            post(5)
            for t, n in TT:
                for kk in range(2):
                    b = 2 * t + kk
                    dve.wait_ge(aux_done, AUX_END + b + 1)
                    dve.tensor_copy(xt[0:n, t, kk * 512:(kk + 1) * 512], aux[2 + b % 2][0:n, :]).then_inc(out_copied, 1)


_OUTS = [("y_prompt", (1, 512, 1024)), ("y_sample", (8, 4, 1024)), ("pool_prompt", (1, 1, 15, 1024)),
         ("conv_prompt", (1, 1, 3, 4096)), ("delta_prompt", (1, 1, 16, 128, 128)), ("pool_sample", (1, 8, 15, 1024)),
         ("conv_sample", (1, 8, 3, 4096)), ("delta_sample", (1, 8, 16, 128, 128))]


def shape_constants():
    c = np.zeros((P, 1448), np.float32)
    i, j = np.arange(P)[:, None], np.arange(P)[None, :]
    c[:, 0:128] = np.eye(P)
    c[:, 128:256] = 1.0 / D
    for g, w in enumerate((2, 4, 8, 16)):
        c[:, 256 + 16 * g:256 + 16 * (g + 1)] = w / np.minimum(np.arange(16) + 1, w)
    c[:, 320:448] = 1.0
    c[:, 448:576] = i <= j
    c[:, 576:704] = np.where(j > i, 1e30, 0.0)
    c[:, 704:832] = j < i
    c[:, 832:960] = -1.0 * (i // 2 == j // 2)
    for n in range(LEVELS):
        half = 2 << n
        second = np.arange(P)[(np.arange(P) // half) % 2 == 1]
        c[:, 960 + 64 * n:1024 + 64 * n] = i // half == second[None, :] // half - 1
    s, t = i[0:32], j[:, 0:32]
    same = s // NS == t // NS
    c[0:32, 1344:1376] = same & (s <= t)
    c[0:32, 1376:1408] = same
    c[0:32, 1408:1440] = np.where(same & (t <= s), 0.0, 1e30)
    for b in range(NB):
        c[0:32, 1440 + b] = np.arange(32) // NS == b
    return c


def kernel(**inputs):
    import numpy as _np
    import concourse.bacc as _bacc
    from concourse import mybir as _mybir
    from concourse.bass_utils import run_bass_kernel_spmd as _run

    nc = _bacc.Bacc("TRN2", target_bir_lowering=False, num_devices=1)
    arrays, ins, outs = {}, {}, {}
    given = dict(inputs)
    given["shape_consts"] = shape_constants()
    for name, a in given.items():
        a = _np.ascontiguousarray(a)
        arrays[f"in_{name}_dram"] = a
        ins[name] = nc.dram_tensor(f"in_{name}_dram", a.shape, _mybir.dt.from_np(a.dtype), kind="ExternalInput").ap()
    for name, shape in _OUTS:
        outs[name] = nc.dram_tensor(f"out_{name}_dram", shape, _mybir.dt.float32, kind="ExternalOutput").ap()
    build(nc, ins.pop("shape_consts"), ins, outs)
    r = _run(nc, [arrays], core_ids=[0])
    return tuple(r.results[0][f"out_{name}_dram"] for name in outs)
```
